# Optimizing a Trainium2 kernel written in Bass

```python
import jax, jax.numpy as jnp
from jax import lax
import numpy as np

D_MODEL = 1024
BATCH = 1
SEQ = 1024
DEPTH = 2

ML_HEADS = 4
ML_DK = 64
ML_DV = 128
ML_CHUNK = 64
CONV_K = 4
GLA_HEADS = 4
GLA_DK = 64
GLA_DV = 128
GLA_CHUNK = 64
GLA_LOWRANK = 16
GLA_TAU = 16.0
ML_QK_W = ML_HEADS * ML_DK
ML_V_W = ML_HEADS * ML_DV
GLA_QK_W = GLA_HEADS * GLA_DK
GLA_V_W = GLA_HEADS * GLA_DV
AB_SPLITS = (2 * ML_QK_W, ML_V_W, ML_V_W, ML_HEADS, ML_HEADS, GLA_QK_W, GLA_QK_W, GLA_V_W, GLA_V_W, GLA_LOWRANK)
AB_IN = sum(AB_SPLITS)
AB_OUT = ML_V_W + GLA_V_W
SWA_Q_HEADS = 16
SWA_KV_HEADS = 2
SWA_HEAD_DIM = 64
SWA_GROUP = SWA_Q_HEADS // SWA_KV_HEADS
WINDOW = 128
ROT_DIM = SWA_HEAD_DIM // 4
ROPE_THETA = 500000.0
QKV_W = (SWA_Q_HEADS + 2 * SWA_KV_HEADS) * SWA_HEAD_DIM
N_GROUPS = 4
EXPERTS_PER_GROUP = 8
N_EXPERTS = N_GROUPS * EXPERTS_PER_GROUP
TOP_K = 2
D_FF_EXPERT = 512
MOE_BLOCK = 128
EPS = 1e-6

kernel_name = "hybrid_mlstm_gla_swa_hmoe"

F32 = jnp.float32

def rmsnorm(x, g):
    x32 = x.astype(F32)
    y = x32 * lax.rsqrt(jnp.mean(x32 * x32, axis=-1, keepdims=True) + EPS)
    return (y * g.astype(F32)).astype(x.dtype)

def causal_depthwise_conv(x, w, b):
    y = lax.conv_general_dilated(x, w[:, None, :], window_strides=(1,), padding=[(CONV_K - 1, 0)],
                                 dimension_numbers=('NWC', 'WIO', 'NWC'), feature_group_count=x.shape[-1])
    return y + b

def to_chunks(t, size):
    b, s, h, d = t.shape
    return t.reshape(b, s // size, size, h, d).transpose(0, 3, 1, 2, 4)

def from_chunks(t):
    b, h, nc, l, d = t.shape
    return t.transpose(0, 2, 3, 1, 4).reshape(b, nc * l, h, d)

def mlstm_chunkwise(q, k, v, i_pre, f_pre):
    L = ML_CHUNK
    q = to_chunks(q.astype(F32), L)
    k = to_chunks(k.astype(F32), L) * (ML_DK ** -0.5)
    v = to_chunks(v.astype(F32), L)
    ig = to_chunks(i_pre.astype(F32)[..., None], L)[..., 0]
    logf = jax.nn.log_sigmoid(to_chunks(f_pre.astype(F32)[..., None], L)[..., 0])
    bcum = jnp.cumsum(logf, axis=-1)
    g = bcum[..., -1]
    a = g[..., None] - bcum + ig
    a_max = jnp.max(a, axis=-1)
    wa = jnp.exp(a - a_max[..., None])
    c_chunk = jnp.einsum('bhcs,bhcsk,bhcsv->bhckv', wa, k, v)
    n_chunk = jnp.einsum('bhcs,bhcsk->bhck', wa, k)

    def step(carry, xs):
        c_st, n_st, m_st = carry
        cc, nc, am, gc = xs
        m_new = jnp.maximum(gc + m_st, am)
        s_old = jnp.exp(gc + m_st - m_new)
        s_in = jnp.exp(am - m_new)
        c_new = s_old[..., None, None] * c_st + s_in[..., None, None] * cc
        n_new = s_old[..., None] * n_st + s_in[..., None] * nc
        return (c_new, n_new, m_new), (c_st, n_st, m_st)

    bsz, nh, _, _, dk = k.shape
    dv = v.shape[-1]
    init = (jnp.zeros((bsz, nh, dk, dv), F32), jnp.zeros((bsz, nh, dk), F32), jnp.full((bsz, nh), -jnp.inf, F32))
    mv = lambda t: jnp.moveaxis(t, 2, 0)
    _, (c_prev, n_prev, m_prev) = lax.scan(step, init, (mv(c_chunk), mv(n_chunk), mv(a_max), mv(g)))
    c_prev = jnp.moveaxis(c_prev, 0, 2)
    n_prev = jnp.moveaxis(n_prev, 0, 2)
    m_prev = jnp.moveaxis(m_prev, 0, 2)

    causal = jnp.tril(jnp.ones((L, L), dtype=bool))
    d_log = jnp.where(causal, bcum[..., :, None] - bcum[..., None, :] + ig[..., None, :], -jnp.inf)
    inter_log = bcum + m_prev[..., None]
    m_t = jnp.maximum(inter_log, jnp.max(d_log, axis=-1))
    s_inter = jnp.exp(inter_log - m_t)
    qk = jnp.einsum('bhctk,bhcsk->bhcts', q, k) * jnp.exp(d_log - m_t[..., None])
    num = s_inter[..., None] * jnp.einsum('bhctk,bhckv->bhctv', q, c_prev) + jnp.einsum('bhcts,bhcsv->bhctv', qk, v)
    den = s_inter * jnp.einsum('bhctk,bhck->bhct', q, n_prev) + jnp.sum(qk, axis=-1)
    h = num / jnp.maximum(jnp.abs(den), jnp.exp(-m_t))[..., None]
    return from_chunks(h)

def gla_chunkwise(q, k, v, log_alpha):
    L = GLA_CHUNK
    q = to_chunks(q.astype(F32), L)
    k = to_chunks(k.astype(F32), L) * (GLA_DK ** -0.5)
    v = to_chunks(v.astype(F32), L)
    bcum = jnp.cumsum(to_chunks(log_alpha.astype(F32), L), axis=3)
    g = bcum[..., -1, :]
    q_dec = q * jnp.exp(bcum)
    k_inv = k * jnp.exp(-bcum)
    k_end = k * jnp.exp(g[..., None, :] - bcum)
    s_chunk = jnp.einsum('bhcsk,bhcsv->bhckv', k_end, v)

    def step(s, xs):
        sc, gc = xs
        return jnp.exp(gc)[..., None] * s + sc, s

    bsz, nh, _, _, dk = k.shape
    dv = v.shape[-1]
    mv = lambda t: jnp.moveaxis(t, 2, 0)
    _, s_prev = lax.scan(step, jnp.zeros((bsz, nh, dk, dv), F32), (mv(s_chunk), mv(g)))
    s_prev = jnp.moveaxis(s_prev, 0, 2)
    causal = jnp.tril(jnp.ones((L, L), dtype=bool))
    att = jnp.where(causal, jnp.einsum('bhctk,bhcsk->bhcts', q_dec, k_inv), 0.0)
    o = jnp.einsum('bhctk,bhckv->bhctv', q_dec, s_prev) + jnp.einsum('bhcts,bhcsv->bhctv', att, v)
    return from_chunks(o)

def mlstm_gla_mixer(u, w_in, conv_w, conv_b, ig_b, fg_b, ml_norm, lr_up, gate_b, gla_norm, w_out):
    bsz, s, _ = u.shape
    idx = np.cumsum(AB_SPLITS)[:-1].tolist()
    (ml_qk, ml_v, ml_o, ml_i, ml_f, gq, gk, gv, gg, glr) = jnp.split(u @ w_in, idx, axis=-1)
    ml_qk = jax.nn.silu(causal_depthwise_conv(ml_qk, conv_w, conv_b))
    ml_q, ml_k = jnp.split(ml_qk, 2, axis=-1)
    ml_h = mlstm_chunkwise(ml_q.reshape(bsz, s, ML_HEADS, ML_DK), ml_k.reshape(bsz, s, ML_HEADS, ML_DK),
                           ml_v.reshape(bsz, s, ML_HEADS, ML_DV), ml_i + ig_b, ml_f + fg_b)
    mu = jnp.mean(ml_h, axis=-1, keepdims=True)
    ml_h = (ml_h - mu) * lax.rsqrt(jnp.mean(jnp.square(ml_h - mu), axis=-1, keepdims=True) + EPS)
    ml_out = ml_h.reshape(bsz, s, ML_V_W) * ml_norm.astype(F32) * jax.nn.sigmoid(ml_o.astype(F32))
    log_alpha = jax.nn.log_sigmoid((glr @ lr_up + gate_b).astype(F32)) / GLA_TAU
    gla_h = gla_chunkwise(gq.reshape(bsz, s, GLA_HEADS, GLA_DK), gk.reshape(bsz, s, GLA_HEADS, GLA_DK),
                          gv.reshape(bsz, s, GLA_HEADS, GLA_DV), log_alpha.reshape(bsz, s, GLA_HEADS, GLA_DK))
    gla_h = gla_h * lax.rsqrt(jnp.mean(gla_h * gla_h, axis=-1, keepdims=True) + EPS)
    gla_out = gla_h.reshape(bsz, s, GLA_V_W) * gla_norm.astype(F32) * jax.nn.silu(gg.astype(F32))
    y = jnp.concatenate([ml_out, gla_out], axis=-1).astype(u.dtype)
    return y @ w_out

def partial_rotary(t, cos, sin):
    half = ROT_DIM // 2
    t1 = t[..., :half].astype(F32)
    t2 = t[..., half:ROT_DIM].astype(F32)
    rot = jnp.concatenate([t1 * cos - t2 * sin, t2 * cos + t1 * sin], axis=-1).astype(t.dtype)
    return jnp.concatenate([rot, t[..., ROT_DIM:]], axis=-1)

def swa_sink_attention(u, positions, w_qkv, b_qkv, sinks, w_o, b_o):
    bsz, s, _ = u.shape
    q, k, v = jnp.split(u @ w_qkv + b_qkv, [SWA_Q_HEADS * SWA_HEAD_DIM, (SWA_Q_HEADS + SWA_KV_HEADS) * SWA_HEAD_DIM], axis=-1)
    q = q.reshape(bsz, s, SWA_Q_HEADS, SWA_HEAD_DIM)
    k = k.reshape(bsz, s, SWA_KV_HEADS, SWA_HEAD_DIM)
    v = v.reshape(bsz, s, SWA_KV_HEADS, SWA_HEAD_DIM)
    inv_freq = ROPE_THETA ** (-jnp.arange(0, ROT_DIM, 2, dtype=F32) / ROT_DIM)
    ang = positions.astype(F32)[..., None] * inv_freq
    cos, sin = jnp.cos(ang)[:, :, None, :], jnp.sin(ang)[:, :, None, :]
    q = partial_rotary(q, cos, sin)
    k = partial_rotary(k, cos, sin)
    nb = s // WINDOW
    qb = q.reshape(bsz, nb, WINDOW, SWA_KV_HEADS, SWA_GROUP, SWA_HEAD_DIM)
    kb = k.reshape(bsz, nb, WINDOW, SWA_KV_HEADS, SWA_HEAD_DIM)
    vb = v.reshape(bsz, nb, WINDOW, SWA_KV_HEADS, SWA_HEAD_DIM)
    prev = lambda t: jnp.concatenate([jnp.zeros_like(t[:, :1]), t[:, :-1]], axis=1)
    kk = jnp.concatenate([prev(kb), kb], axis=2)
    vv = jnp.concatenate([prev(vb), vb], axis=2)
    scores = jnp.einsum('bnqhgd,bnkhd->bnhgqk', qb, kk, preferred_element_type=F32) * (SWA_HEAD_DIM ** -0.5)
    qi = jnp.arange(WINDOW)[:, None] + WINDOW
    kj = jnp.arange(2 * WINDOW)[None, :]
    rel = qi - kj
    valid = ((rel >= 0) & (rel < WINDOW))[None] & ((jnp.arange(nb)[:, None, None] > 0) | (kj[None] >= WINDOW))
    scores = jnp.where(valid[None, :, None, None], scores, -jnp.inf)
    sink = sinks.astype(F32).reshape(SWA_KV_HEADS, SWA_GROUP)[None, None, :, :, None]
    m = jnp.maximum(jnp.max(scores, axis=-1), sink)
    p = jnp.exp(scores - m[..., None])
    denom = jnp.sum(p, axis=-1) + jnp.exp(sink - m)
    o = jnp.einsum('bnhgqk,bnkhd->bnhgqd', p, vv.astype(F32)) / denom[..., None]
    o = o.transpose(0, 1, 4, 2, 3, 5).reshape(bsz, s, SWA_Q_HEADS * SWA_HEAD_DIM).astype(u.dtype)
    return o @ w_o + b_o

def hierarchical_moe(u, wg, bg, we, be, w_gate, w_up, w_down):
    bsz, s, d = u.shape
    t = bsz * s
    xt = u.reshape(t, d)
    g_probs = jax.nn.softmax((xt @ wg).astype(F32) + bg.astype(F32), axis=-1)
    g_p, g_idx = lax.top_k(g_probs, 1)
    e_logits = ((xt @ we).astype(F32) + be.astype(F32)).reshape(t, N_GROUPS, EXPERTS_PER_GROUP)
    e_in_group = jnp.take_along_axis(e_logits, g_idx[:, :, None], axis=1)[:, 0]
    top_l, top_i = lax.top_k(e_in_group, TOP_K)
    gates = g_p * jax.nn.softmax(top_l, axis=-1)
    expert_ids = g_idx * EXPERTS_PER_GROUP + top_i
    n_assign = t * TOP_K
    n_blocks = (n_assign + MOE_BLOCK - 1) // MOE_BLOCK + N_EXPERTS
    n_pad = n_blocks * MOE_BLOCK
    flat_e = expert_ids.reshape(-1)
    flat_tok = jnp.repeat(jnp.arange(t, dtype=jnp.int32), TOP_K)
    flat_w = gates.reshape(-1)
    order = jnp.argsort(flat_e)
    e_sorted = flat_e[order]
    counts = jnp.bincount(flat_e, length=N_EXPERTS)
    padded = (counts + MOE_BLOCK - 1) // MOE_BLOCK * MOE_BLOCK
    pad_end = jnp.cumsum(padded)
    pad_start = pad_end - padded
    start = jnp.cumsum(counts) - counts
    dest = pad_start[e_sorted] + jnp.arange(n_assign, dtype=jnp.int32) - start[e_sorted]
    tok_buf = jnp.zeros((n_pad,), jnp.int32).at[dest].set(flat_tok[order])
    w_buf = jnp.zeros((n_pad,), F32).at[dest].set(flat_w[order])
    block_expert = jnp.minimum(jnp.searchsorted(pad_end, jnp.arange(n_blocks, dtype=jnp.int32) * MOE_BLOCK, side='right'), N_EXPERTS - 1)
    x_buf = xt[tok_buf].reshape(n_blocks, MOE_BLOCK, d)

    def expert_block(args):
        xb, e = args
        return (jax.nn.silu(xb @ w_gate[e]) * (xb @ w_up[e])) @ w_down[e]

    y_buf = lax.map(expert_block, (x_buf, block_expert)).reshape(n_pad, d)
    out = jnp.zeros((t, d), F32).at[tok_buf].add(y_buf.astype(F32) * w_buf[:, None])
    return out.astype(u.dtype).reshape(bsz, s, d)

def setup_inputs(seed: int = 0) -> dict:
    key = jax.random.key(seed)
    ks = jax.random.split(key, 32)
    n_even = (DEPTH + 1) // 2
    n_odd = DEPTH // 2
    nrm = lambda k, shape, scale: jax.random.normal(k, shape, F32) * scale
    gain = lambda k, shape: 1.0 + 0.02 * jax.random.normal(k, shape, F32)
    offset = jax.random.randint(ks[1], (BATCH, 1), 0, 4096, dtype=jnp.int32)
    positions = offset + jnp.arange(SEQ, dtype=jnp.int32)[None, :]
    fgate_b = jnp.linspace(3.0, 6.0, ML_HEADS, dtype=F32)[None, :] + 0.1 * jax.random.normal(ks[9], (n_even, ML_HEADS), F32)
    return {
        "x": nrm(ks[0], (BATCH, SEQ, D_MODEL), 1.0),
        "positions": positions,
        "mix_norm": gain(ks[2], (DEPTH, D_MODEL)),
        "ffn_norm": gain(ks[3], (DEPTH, D_MODEL)),
        "final_norm": gain(ks[4], (D_MODEL,)),
        "ab_w_in": nrm(ks[5], (n_even, D_MODEL, AB_IN), D_MODEL ** -0.5),
        "ab_conv_w": nrm(ks[6], (n_even, CONV_K, 2 * ML_QK_W), CONV_K ** -0.5),
        "ab_conv_b": nrm(ks[7], (n_even, 2 * ML_QK_W), 0.02),
        "ml_igate_b": nrm(ks[8], (n_even, ML_HEADS), 0.1),
        "ml_fgate_b": fgate_b,
        "ml_head_norm": gain(ks[10], (n_even, ML_V_W)),
        "gla_w_lr_up": nrm(ks[11], (n_even, GLA_LOWRANK, GLA_QK_W), GLA_LOWRANK ** -0.5),
        "gla_gate_b": nrm(ks[12], (n_even, GLA_QK_W), 0.1),
        "gla_head_norm": gain(ks[13], (n_even, GLA_V_W)),
        "ab_w_out": nrm(ks[14], (n_even, AB_OUT, D_MODEL), AB_OUT ** -0.5),
        "swa_w_qkv": nrm(ks[15], (n_odd, D_MODEL, QKV_W), D_MODEL ** -0.5),
        "swa_b_qkv": nrm(ks[16], (n_odd, QKV_W), 0.02),
        "swa_sinks": nrm(ks[17], (n_odd, SWA_Q_HEADS), 0.5),
        "swa_w_o": nrm(ks[18], (n_odd, SWA_Q_HEADS * SWA_HEAD_DIM, D_MODEL), (SWA_Q_HEADS * SWA_HEAD_DIM) ** -0.5),
        "swa_b_o": nrm(ks[19], (n_odd, D_MODEL), 0.02),
        "router_group_w": nrm(ks[20], (DEPTH, D_MODEL, N_GROUPS), D_MODEL ** -0.5),
        "router_group_b": nrm(ks[21], (DEPTH, N_GROUPS), 0.01),
        "router_expert_w": nrm(ks[22], (DEPTH, D_MODEL, N_EXPERTS), D_MODEL ** -0.5),
        "router_expert_b": nrm(ks[23], (DEPTH, N_EXPERTS), 0.01),
        "expert_w_gate": nrm(ks[24], (DEPTH, N_EXPERTS, D_MODEL, D_FF_EXPERT), D_MODEL ** -0.5),
        "expert_w_up": nrm(ks[25], (DEPTH, N_EXPERTS, D_MODEL, D_FF_EXPERT), D_MODEL ** -0.5),
        "expert_w_down": nrm(ks[26], (DEPTH, N_EXPERTS, D_FF_EXPERT, D_MODEL), D_FF_EXPERT ** -0.5),
    }

def reference(x, positions, mix_norm, ffn_norm, final_norm, ab_w_in, ab_conv_w, ab_conv_b, ml_igate_b, ml_fgate_b,
              ml_head_norm, gla_w_lr_up, gla_gate_b, gla_head_norm, ab_w_out, swa_w_qkv, swa_b_qkv, swa_sinks,
              swa_w_o, swa_b_o, router_group_w, router_group_b, router_expert_w, router_expert_b,
              expert_w_gate, expert_w_up, expert_w_down):
    h = x
    for layer in range(DEPTH):
        j = layer // 2
        u = rmsnorm(h, mix_norm[layer])
        if layer % 2 == 0:
            mix = mlstm_gla_mixer(u, ab_w_in[j], ab_conv_w[j], ab_conv_b[j], ml_igate_b[j], ml_fgate_b[j],
                                  ml_head_norm[j], gla_w_lr_up[j], gla_gate_b[j], gla_head_norm[j], ab_w_out[j])
        else:
            mix = swa_sink_attention(u, positions, swa_w_qkv[j], swa_b_qkv[j], swa_sinks[j], swa_w_o[j], swa_b_o[j])
        h = h + mix.astype(h.dtype)
        u = rmsnorm(h, ffn_norm[layer])
        h = h + hierarchical_moe(u, router_group_w[layer], router_group_b[layer], router_expert_w[layer],
                                 router_expert_b[layer], expert_w_gate[layer], expert_w_up[layer],
                                 expert_w_down[layer]).astype(h.dtype)
    return rmsnorm(h, final_norm)


_drawn_inputs = setup_inputs


def setup_inputs(seed=0):
    import zlib

    import numpy as np

    out = dict(_drawn_inputs(seed))
    spreads = {}
    factors = {'final_norm': 8.272, 'ml_igate_b': 64.0, 'swa_sinks': 8.0, 'router_group_b': 17.244}
    for name, (base, spread) in spreads.items():
        noise = np.random.default_rng([zlib.crc32(name.encode()), seed]).standard_normal(out[name].shape)
        drawn = base * np.exp(spread * noise) if base else spread * noise
        out[name] = __import__('jax').numpy.asarray(drawn.astype(out[name].dtype))
    for name, factor in factors.items():
        out[name] = (out[name] * factor).astype(out[name].dtype)
    return out
```

```python
from contextlib import ExitStack

import concourse.bass as bass
from concourse import mybir

F32 = mybir.dt.float32
F32R = mybir.dt.float32r
I32 = mybir.dt.int32
U32 = mybir.dt.uint32
ALU = mybir.AluOpType
ACT = mybir.ActivationFunctionType
AX = mybir.AxisListType
ds = bass.ds

P = 128
BANK = 512
EPS = 1e-6
NEG = -1e30
ML_HEADS, GLA_HEADS, DK, DV = 4, 4, 64, 128
CONV_K = 4
LOWRANK = 16
GLA_CHUNK = 64
GLA_TAU = 16.0
Q_HEADS, KV_HEADS, HEAD_DIM, WINDOW = 16, 2, 64, 128
ROT = HEAD_DIM // 4
ROPE_THETA = 500000.0
N_GROUPS, PER_GROUP, TOP_K = 4, 8, 2
N_EXPERTS = N_GROUPS * PER_GROUP


def bc(ap, axis, n):
    a = ap.unsqueeze(axis)
    shape = list(a.shape)
    shape[axis] = n
    return a.broadcast_to(shape)


class Memory:

    def __init__(self, nc, ctx, prefix):
        self.nc, self.ctx, self.prefix, self.sems = nc, ctx, prefix, []
        ctx.callback(self.clear)

    def clear(self):
        if self.sems:
            self.nc.clear_and_free_semaphores(self.sems)
            self.nc.all_engine_barrier()

    def sb(self, name, shape, dtype=F32):
        return self.ctx.enter_context(self.nc.sbuf_tensor(f"{self.prefix}_{name}", shape, dtype))

    def ps(self, name, shape, dtype=F32):
        return self.ctx.enter_context(self.nc.psum_tensor(f"{self.prefix}_{name}", shape, dtype))

    def sem(self, name):
        self.sems.append(self.nc.alloc_semaphore(f"{self.prefix}_{name}"))
        return self.sems[-1]


def broadcast_row(dram_row, n):
    return dram_row.rearrange("(a n) -> a n", a=1).broadcast_to([n, dram_row.shape[0]])


def make_constants(nc, mem, A):
    c = {}
    for name, shape, dt in (
        ("ident", [P, P], F32), ("ones", [P, P], F32), ("tri", [P, P], F32), ("tri_strict", [P, P], F32),
        ("tri_gla", [P, P], F32), ("causal_add", [P, P], F32), ("last_row", [P, P], F32),
        ("gla_mask", [P, P], F32), ("swa_add", [P, 2, P], F32),
        ("iota", [P, P], F32), ("token2", [P, 8], F32), ("eps", [P, 1], F32),
        ("by_channel", [P, 60], F32), ("channel_rows", [60, P], F32),
        ("gate_bias", [P, 8], F32), ("sinks", [P, Q_HEADS], F32),
        ("lr_up", [LOWRANK + 1, GLA_HEADS * DK], F32), ("router_b", [P, 2, 36], F32),
    ):
        c[name] = mem.sb(name, shape, dt)
    params = [("mix_gain0", A["mix_norm"][0], 8), ("mix_gain1", A["mix_norm"][1], 8), ("ffn_gain0", A["ffn_norm"][0], 8),
              ("ffn_gain1", A["ffn_norm"][1], 8), ("ml_gain", A["ml_head_norm"][0], 4), ("gla_gain", A["gla_head_norm"][0], 4),
              ("conv_b", A["ab_conv_b"][0], 4)] + [(f"conv_w{j}", A["ab_conv_w"][0, j], 4) for j in range(CONV_K)]
    at = 0
    row_loads = []
    for name, src, n in params:
        row_loads.append((c["channel_rows"][at:at + n, :], src.rearrange("(k p) -> k p", p=P)))
        c[name] = c["by_channel"][:, at:at + n]
        if name == "ml_gain":
            c["y_gain"] = c["by_channel"][:, at:at + 8]
        at += n
    loaded, filled = mem.sem("loaded"), mem.sem("filled")
    with nc.Block() as block:

        @block.sync
        def _(sp):
            loads = row_loads + [
                (c["gate_bias"][:, 0:4], broadcast_row(A["ml_igate_b"][0], P)),
                (c["gate_bias"][:, 4:8], broadcast_row(A["ml_fgate_b"][0], P)),
                (c["sinks"][:], broadcast_row(A["swa_sinks"][0], P)),
                (c["lr_up"][0:LOWRANK, :], A["gla_w_lr_up"][0]),
                (c["lr_up"][LOWRANK:LOWRANK + 1, :], A["gla_gate_b"]),
            ]
            for layer in range(2):
                loads.append((c["router_b"][:, layer, 0:4], broadcast_row(A["router_group_b"][layer], P)))
                loads.append((c["router_b"][:, layer, 4:36], broadcast_row(A["router_expert_b"][layer], P)))
            for dst, src in loads:
                sp.dma_start(dst, src).then_inc(loaded, 16)
            sp.wait_ge(loaded, 16 * len(loads))

        @block.gpsimd
        def _(pool):
            for name, value in (("ident", 0.0), ("ones", 1.0), ("tri", 1.0), ("tri_strict", 1.0), ("tri_gla", 1.0 / GLA_TAU),
                                ("causal_add", 0.0), ("last_row", 0.0), ("gla_mask", 1.0), ("swa_add", 0.0), ("eps", EPS)):
                nc.gpsimd.memset(c[name][:], value)
            nc.gpsimd.iota(c["iota"][:], pattern=[[1, P]], base=0, channel_multiplier=0, allow_small_or_imprecise_dtypes=True)
            nc.gpsimd.iota(c["token2"][:], pattern=[[2 * P, 8]], base=0, channel_multiplier=2, allow_small_or_imprecise_dtypes=True)
            pool.drain()
            down, up = ([[-1, P]], 1), ([[1, P]], -1)
            for name, (pattern, step), op, fill in (
                ("ident", down, ALU.not_equal, 1.0), ("tri", up, ALU.is_ge, 0.0), ("tri_strict", up, ALU.is_gt, 0.0),
                ("tri_gla", up, ALU.is_ge, 0.0), ("gla_mask", up, ALU.is_ge, 0.0), ("causal_add", down, ALU.is_ge, NEG),
            ):
                nc.gpsimd.affine_select(out=c[name][:], in_=c[name][:], pattern=pattern, compare_op=op, fill=fill,
                                        base=0, channel_multiplier=step)
            nc.gpsimd.affine_select(out=c["last_row"][:], in_=c["last_row"][:], pattern=[[0, P]], compare_op=ALU.is_gt,
                                    fill=1.0, base=P - 1, channel_multiplier=-1)
            for slot, (pattern, step), op in ((0, up, ALU.is_gt), (1, down, ALU.is_ge)):
                part = c["swa_add"][:, slot]
                nc.gpsimd.affine_select(out=part, in_=part, pattern=pattern, compare_op=op, fill=NEG,
                                        base=0, channel_multiplier=step)
            pool.drain()
            nc.gpsimd.memset(c["tri_gla"][0:GLA_CHUNK, GLA_CHUNK:P], 0.0)
            nc.gpsimd.memset(c["gla_mask"][0:GLA_CHUNK, GLA_CHUNK:P], 0.0)

    with ExitStack() as ctx, nc.Block() as block:
        turned = ctx.enter_context(nc.psum_tensor("by_channel_turned", [P, 60], F32))

        @block.tensor
        def _(pe):
            nc.tensor.transpose(turned[:], c["channel_rows"][:], c["ident"][0:60, 0:60]).then_inc(filled, 1)

        @block.vector
        def _(dve):
            dve.wait_ge(filled, 1)
            nc.vector.tensor_copy(c["by_channel"][:], turned[:])
    return c


def project_tiles(nc, prefix, c, rows_of, gain, weights, n_cols, take, weights_ready=None, store=None, store_engine=None):
    with ExitStack() as ctx:
        mem = Memory(nc, ctx, prefix)
        rows = [mem.sb(f"rows{j}", [P, 1024]) for j in range(2)]
        cols = [mem.sb(f"cols{j}", [P, 8, P]) for j in range(2)]
        turned = [mem.ps(f"turned{j}", [P, 8, P]) for j in range(2)]
        n_banks = (n_cols + BANK - 1) // BANK
        slots = 4 // n_banks
        product = [mem.ps(f"product{j}", [P, n_banks * BANK]) for j in range(slots)]
        rows_ready, rows_free, turned_ready, turned_free = (mem.sem(x) for x in ("rows_ready", "rows_free", "turned_ready", "turned_free"))
        cols_ready, product_ready, product_free = (mem.sem(x) for x in ("cols_ready", "product_ready", "product_free"))
        stored = [mem.sem(f"stored{j}") for j in range(2)]
        with nc.Block() as block:

            @block.scalar
            def _(act):
                with act.Fori(0, 4) as pair:
                    for j in range(2):
                        act.wait_ge(rows_free, 2 * pair + j + 1)
                        if store is not None:
                            act.wait_ge(stored[j], 16 * pair)
                        rows_of(act, 2 * pair + j, rows[j][:]).then_inc(rows_ready, 1)

            if store is not None:

                @block.sync
                def _(sp):
                    with sp.Fori(0, 4) as pair:
                        for j in range(2):
                            sp.wait_ge(rows_ready, 2 * pair + j + 1)
                            sp.dma_start(store[ds((2 * pair + j) * P, P), :], rows[j][:]).then_inc(stored[j], 16)
                    for j in range(2):
                        sp.wait_ge(stored[j], 16 * 4)

            @block.tensor
            def _(pe):
                pe.sem_inc(rows_free, 2)

                def turn(tile, j):
                    pe.wait_ge(rows_ready, tile + 1)
                    pe.wait_ge(turned_free, tile + 1)
                    for k in range(8):
                        last = nc.tensor.transpose(turned[j][:, k], rows[j][:, k * P:(k + 1) * P], c["ident"][:])
                    last.then_inc(turned_ready, 1)
                    pe.wait_ge(turned_ready, tile + 1)
                    pe.sem_inc(rows_free, 1)

                def multiply(tile, j):
                    pe.wait_ge(cols_ready, tile + 1)
                    pe.wait_ge(product_free, tile + 1)
                    for b in range(n_banks):
                        w = min(BANK, n_cols - b * BANK)
                        for k in range(8):
                            last = nc.tensor.matmul(product[j % slots][:, b * BANK:b * BANK + w], cols[j][:, k],
                                                    weights[:, k, b * BANK:b * BANK + w], start=(k == 0), stop=(k == 7))
                    last.then_inc(product_ready, 1)

                turn(0, 0)
                if weights_ready is not None:
                    pe.wait_ge(*weights_ready)
                with pe.Fori(0, 3) as pair:
                    for j in range(2):
                        turn(2 * pair + j + 1, 1 - j)
                        multiply(2 * pair + j, j)
                turn(7, 1)
                multiply(6, 0)
                multiply(7, 1)

            @block.vector
            def _(dve):
                dve.sem_inc(turned_free, 2)
                dve.sem_inc(product_free, slots)

                def evacuate(tile, j):
                    dve.wait_ge(turned_ready, tile + 1)
                    for half in range(2):
                        src, dst = turned[j][:, 4 * half:4 * half + 4], cols[j][:, 4 * half:4 * half + 4]
                        if gain is None:
                            last = nc.vector.tensor_copy(dst, src)
                        else:
                            last = nc.vector.tensor_tensor(dst, src, bc(gain[:, 4 * half:4 * half + 4], 2, P), ALU.mult)
                    last.then_inc(cols_ready, 1)
                    dve.drain()
                    dve.sem_inc(turned_free, 1)

                def consume(tile, j):
                    dve.wait_ge(product_ready, tile + 1)
                    take(dve, tile, product[j % slots])
                    dve.drain()
                    dve.sem_inc(product_free, 1)

                evacuate(0, 0)
                with dve.Fori(0, 3) as pair:
                    for j in range(2):
                        evacuate(2 * pair + j + 1, 1 - j)
                        consume(2 * pair + j, j)
                evacuate(7, 1)
                consume(6, 0)
                consume(7, 1)


def row_scales(nc, prefix, c, h, out, loads=None):
    with ExitStack() as ctx:
        mem = Memory(nc, ctx, prefix)
        junk, sums, root = mem.sb("junk", [P, 1024]), mem.sb("sums", [P, 8]), mem.sb("root", [P, 8])
        squared, rooted = mem.sem("squared"), mem.sem("rooted")
        with nc.Block() as block:
            if loads is not None:

                @block.sync
                def _(sp):
                    loads(sp)

            @block.scalar
            def _(act):
                with act.Fori(0, 8) as tile:
                    nc.scalar.activation(junk[:], h[:, tile], ACT.Square, accum_out=sums[:, ds(tile, 1)]).then_inc(squared, 1)
                    act.wait_ge(squared, tile + 1)
                nc.scalar.activation(root[:], sums[:], ACT.Sqrt, bias=c["eps"][:], scale=1.0 / 1024).then_inc(rooted, 1)

            @block.vector
            def _(dve):
                dve.wait_ge(rooted, 1)
                nc.vector.reciprocal(out[:], root[:])


def layer0_inputs(nc, c, A, h, uT, scale):
    with ExitStack() as ctx:
        mem = Memory(nc, ctx, "l0in")
        rows = [mem.sb(f"rows{j}", [P, 1024]) for j in range(2)]
        turned = [mem.ps(f"turned{j}", [P, 8, P]) for j in range(2)]
        rows_ready, turned_ready, cols_ready = mem.sem("rows_ready"), mem.sem("turned_ready"), mem.sem("cols_ready")
        with nc.Block() as block:

            @block.scalar
            def _(act):
                with act.Fori(0, 4) as pair:
                    for j in range(2):
                        act.wait_ge(turned_ready, 2 * pair + j + 1)
                        nc.scalar.activation(rows[j][:], h[:, 2 * pair + j], ACT.Copy,
                                             scale=scale[:, ds(2 * pair + j, 1)]).then_inc(rows_ready, 1)

            @block.tensor
            def _(pe):
                pe.sem_inc(turned_ready, 2)
                with pe.Fori(0, 4) as pair:
                    for j in range(2):
                        pe.wait_ge(rows_ready, 2 * pair + j + 1)
                        pe.wait_ge(cols_ready, 2 * pair + j + 1)
                        for k in range(8):
                            last = nc.tensor.transpose(turned[j][:, k], rows[j][:, k * P:(k + 1) * P], c["ident"][:])
                        last.then_inc(turned_ready, 1)

            @block.vector
            def _(dve):
                dve.sem_inc(cols_ready, 2)
                with dve.Fori(0, 4) as pair:
                    for j in range(2):
                        dve.wait_ge(turned_ready, 2 * pair + j + 3)
                        for half in range(2):
                            last = nc.vector.tensor_tensor(uT[:, 2 * pair + j, 4 * half:4 * half + 4], turned[j][:, 4 * half:4 * half + 4],
                                                           bc(c["mix_gain0"][:, 4 * half:4 * half + 4], 2, P), ALU.mult)
                        last.then_inc(cols_ready, 1)


def layer0_projection(nc, c, A, uT, qk, gqk, values, gates, if_rows, lowrank):
    w = A["ab_w_in"][0].rearrange("(k p) n -> p k n", p=P)
    CH0, V0, IF0, GQ0, GV0, LR0 = 0, 512, 1536, 1544, 2056, 3080
    with ExitStack() as ctx:
        mem = Memory(nc, ctx, "l0proj")
        ring = [mem.sb(f"ring{j}", [P, 8, BANK]) for j in range(2)]
        small = mem.sb("small", [P, 8, 24])
        out = mem.ps("out", [P, 4, BANK])
        gate_out = mem.ps("gate_out", [P, 8, 8])
        lr_out = mem.ps("lr_out", [LOWRANK, 2, BANK])
        w_ready = [mem.sem(f"w_ready{j}") for j in range(2)]
        small_ready, small_made = mem.sem("small_ready"), mem.sem("small_made")
        made, taken, cleared, conv_step = mem.sem("made"), mem.sem("taken"), mem.sem("cleared"), mem.sem("conv_step")
        with nc.Block() as block:

            @block.sync
            def _(sp):
                sp.dma_start(small[:, :, 0:8], w[:, :, IF0:IF0 + 8]).then_inc(small_ready, 16)
                sp.dma_start(small[:, :, 8:24], w[:, :, LR0:LR0 + 16]).then_inc(small_ready, 16)
                sp.dma_start(ring[0][:], w[:, :, CH0:CH0 + BANK]).then_inc(w_ready[0], 16)
                sp.dma_start(ring[1][:], w[:, :, GQ0:GQ0 + BANK]).then_inc(w_ready[1], 16)
                with sp.Fori(0, 2) as mixer:
                    for j in range(2):
                        sp.wait_ge(made, 16 * mixer + 8 * j + 8)
                        sp.dma_start(ring[j][:], w[:, :, ds((GV0 - V0) * mixer + V0 + BANK * j, BANK)]).then_inc(w_ready[j], 16)

            @block.tensor
            def _(pe):
                pe.wait_ge(small_ready, 32)
                for tile in range(8):
                    for k in range(8):
                        nc.tensor.matmul(gate_out[:, tile], uT[:, tile, k], small[:, k, 0:8], start=(k == 0), stop=(k == 7))
                for half in range(2):
                    for k in range(8):
                        last = nc.tensor.matmul(lr_out[:, half], small[:, k, 8:24], uT[:, 4 * half:4 * half + 4, k],
                                                start=(k == 0), stop=(k == 7))
                last.then_inc(small_made, 1)
                for j in range(2):
                    pe.wait_ge(w_ready[j], 16)
                    for n in range(8):
                        m, half = n // 2, n % 2
                        pe.wait_ge(taken, 8 * j + n + 1)
                        for k in range(8):
                            last = nc.tensor.matmul(out[:, n % 4], ring[j][:, k, m * P:(m + 1) * P], uT[:, 4 * half:4 * half + 4, k],
                                                    start=(k == 0), stop=(k == 7))
                        last.then_inc(made, 1)
                with pe.Fori(0, 2) as mixer:
                    for j in range(2):
                        pe.wait_ge(w_ready[j], 16 * mixer + 32)
                        for tile in range(8):
                            pe.wait_ge(taken, 16 * mixer + 17 + 8 * j + tile)
                            for k in range(8):
                                last = nc.tensor.matmul(out[:, tile % 4], uT[:, tile, k], ring[j][:, k],
                                                        start=(k == 0), stop=(k == 7))
                            last.then_inc(made, 1)

            @block.gpsimd
            def _(pool):
                nc.gpsimd.memset(qk[:, :, 0:CONV_K - 1], 0.0)
                nc.gpsimd.memset(lowrank[:], 1.0).then_inc(cleared, 1)

            @block.vector
            def _(dve):
                dve.sem_inc(taken, 4)
                dve.wait_ge(small_made, 1)
                dve.wait_ge(cleared, 1)
                nc.vector.tensor_tensor(if_rows[:], gate_out[:], bc(c["gate_bias"][:], 1, 8), ALU.add)
                for half in range(2):
                    nc.vector.tensor_copy(lowrank[0:LOWRANK, half * BANK:(half + 1) * BANK], lr_out[:, half])
                for j in range(2):
                    for n in range(8):
                        m, half = n // 2, n % 2
                        dve.wait_ge(made, 8 * j + n + 1)
                        dst = qk[:, m, 3 + half * BANK:3 + (half + 1) * BANK] if j == 0 else gqk[:, m, half * BANK:(half + 1) * BANK]
                        nc.vector.tensor_copy(dst, out[:, n % 4]).then_inc(taken, 1)
                with dve.Fori(0, 2) as mixer:
                    for j, dst in enumerate((values, gates)):
                        for tile in range(8):
                            dve.wait_ge(made, 16 * mixer + 17 + 8 * j + tile)
                            nc.vector.tensor_copy(dst[:, mixer, tile], out[:, tile % 4]).then_inc(taken, 1)

    with ExitStack() as ctx:
        mem = Memory(nc, ctx, "conv")
        acc = mem.sb("acc", [P, 4, 1024])
        summed = mem.sem("summed")
        with nc.Block() as block:

            @block.vector
            def _(dve):
                for m in range(4):
                    nc.vector.tensor_scalar(acc[:, m], qk[:, m, 0:1024], c["conv_w0"][:, m:m + 1], c["conv_b"][:, m:m + 1],
                                            ALU.mult, ALU.add)
                    for tap in range(1, CONV_K):
                        dve.drain()
                        last = nc.vector.scalar_tensor_tensor(acc[:, m], qk[:, m, tap:tap + 1024], c[f"conv_w{tap}"][:, m:m + 1],
                                                              acc[:, m], ALU.mult, ALU.add)
                    last.then_inc(summed, 1)

            @block.scalar
            def _(act):
                nc.scalar.activation(gates[:, 0], gates[:, 0], ACT.Sigmoid)
                nc.scalar.activation(gates[:, 1], gates[:, 1], ACT.Silu)
                for m in range(4):
                    act.wait_ge(summed, m + 1)
                    nc.scalar.activation(qk[:, m, 0:1024], acc[:, m], ACT.Silu)


def layer0_mixers(nc, c, qk, gqk, values, if_rows, lowrank, hidden, spread):
    B = BANK
    with ExitStack() as ctx:
        mem = Memory(nc, ctx, "mix")
        small = lambda name: mem.sb(name, [P, 8, 4])
        fabs, lexp, logf, bcum, r = (small(x) for x in ("fabs", "lexp", "logf", "bcum", "r"))
        top, m_prev, big_m, neg_m, carried = (small(x) for x in ("top", "m_prev", "big_m", "neg_m", "carried"))
        floor, s_inter, m_last, k_weight, decay, tmp = (small(x) for x in ("floor", "s_inter", "m_last", "k_weight", "decay", "tmp"))
        diag = mem.sb("diag", [P, 4, P])
        shifted = mem.sb("shifted", [P, 8, 4, P])
        bank = [mem.ps(f"bank{n}", [P, B]) for n in range(8)]
        gates_log, cum_ready, r_ready, diag_ready, spread_ready, seen = (
            mem.sem(x) for x in ("gates_log", "cum_ready", "r_ready", "diag_ready", "spread_ready", "seen"))
        m_ready, m_carried, last_wanted, last_ready, neg_ready, exp_ready = (
            mem.sem(x) for x in ("m_ready", "m_carried", "last_wanted", "last_ready", "neg_ready", "exp_ready"))
        with nc.Block() as block:

            @block.scalar
            def _(act):
                nc.scalar.activation(fabs[:], if_rows[:, :, 4:8], ACT.Abs)
                act.drain()
                nc.scalar.activation(lexp[:], fabs[:], ACT.Exp, scale=-1.0)
                act.drain()
                nc.scalar.activation(lexp[:], lexp[:], ACT.Ln, bias=1.0).then_inc(gates_log, 1)
                act.wait_ge(neg_ready, 1)
                nc.scalar.activation(floor[:], floor[:], ACT.Exp)
                nc.scalar.activation(s_inter[:], s_inter[:], ACT.Exp)
                nc.scalar.activation(k_weight[:], k_weight[:], ACT.Exp)
                nc.scalar.activation(decay[:], decay[:], ACT.Exp)

            @block.tensor
            def _(pe):
                pe.wait_ge(gates_log, 2)
                nc.tensor.matmul(bank[0][:, 0:32], c["tri"][:], logf[:], start=True, stop=True).then_inc(cum_ready, 1)
                with pe.Fori(0, 8) as tile:
                    pe.wait_ge(diag_ready, tile + 1)
                    nc.tensor.matmul(bank[1][:], c["ones"][:], diag[:], start=True, stop=True).then_inc(spread_ready, 1)
                with pe.Fori(0, 8) as tile:
                    pe.wait_ge(m_ready, tile + 1)
                    nc.tensor.matmul(bank[2][:, 0:4], c["last_row"][:], carried[:, tile], start=True, stop=True).then_inc(m_carried, 1)
                pe.wait_ge(last_wanted, 1)
                nc.tensor.matmul(bank[3][:, 0:32], c["last_row"][:], big_m[:], start=True, stop=True).then_inc(last_ready, 1)

            @block.vector
            def _(dve):
                dve.wait_ge(gates_log, 1)
                nc.vector.scalar_tensor_tensor(logf[:], if_rows[:, :, 4:8], 0.0, lexp[:], ALU.min, ALU.subtract).then_inc(gates_log, 1)
                dve.wait_ge(cum_ready, 1)
                nc.vector.tensor_copy(bcum[:].rearrange("p t h -> p (t h)"), bank[0][:, 0:32])
                dve.drain()
                nc.vector.tensor_tensor(r[:], if_rows[:, :, 0:4], bcum[:], ALU.subtract)
                dve.drain()
                with dve.Fori(0, 8) as tile:
                    nc.vector.tensor_tensor(diag[:], bc(c["ident"][:], 1, 4), bc(r[:, tile], 2, P), ALU.mult).then_inc(diag_ready, 1)
                    dve.wait_ge(spread_ready, tile + 1)
                    nc.vector.tensor_tensor(shifted[:, tile], bank[1][:].rearrange("p (h s) -> p h s", h=4), bc(c["causal_add"][:], 1, 4), ALU.add)
                    dve.drain()
                    nc.vector.tensor_reduce(top[:, tile], shifted[:, tile], AX.X, ALU.max)
                nc.vector.memset(m_prev[:, 0], NEG)
                dve.drain()
                with dve.Fori(0, 8) as tile:
                    nc.vector.tensor_tensor(big_m[:, tile], top[:, tile], m_prev[:, tile], ALU.max)
                    dve.drain()
                    nc.vector.tensor_tensor(carried[:, tile], big_m[:, tile], bcum[:, tile], ALU.add).then_inc(m_ready, 1)
                    dve.wait_ge(m_carried, tile + 1)
                    nc.vector.tensor_copy(m_prev[:, ds((tile + 1) % 8, 1)].rearrange("p a h -> p (a h)"), bank[2][:, 0:4])
                    dve.drain()
                nc.vector.memset(m_prev[:, 0], NEG).then_inc(last_wanted, 1)
                dve.wait_ge(last_ready, 1)
                nc.vector.tensor_copy(m_last[:].rearrange("p t h -> p (t h)"), bank[3][:, 0:32])
                nc.vector.tensor_scalar(neg_m[:], big_m[:], -1.0, None, ALU.mult)
                nc.vector.tensor_scalar(floor[:], carried[:], -1.0, None, ALU.mult)
                nc.vector.tensor_tensor(s_inter[:], m_prev[:], big_m[:], ALU.subtract)
                dve.drain()
                nc.vector.tensor_tensor(k_weight[:], r[:], m_last[:], ALU.subtract)
                nc.vector.tensor_tensor(decay[:], m_prev[:], m_last[:], ALU.subtract)
                dve.drain()
                dve.sem_inc(neg_ready, 1)

        state = mem.sb("state", [P, 2, 2 * DV])
        norm_state = mem.sb("norm_state", [P, 2, 2])
        s_even, s_odd = mem.sb("s_even", [P, 2, 2 * DV]), mem.sb("s_odd", [P, 2, 2 * DV])
        qk_t, lr_t = mem.sb("qk_t", [P, 4, P]), mem.sb("lr_t", [LOWRANK + 1, P])
        weight, prob, prob_t = mem.sb("weight", [P, 4, P]), mem.sb("prob", [P, 4, P]), mem.sb("prob_t", [P, 4, P])
        k_rows = mem.sb("k_rows", [P, 4, DK])
        inter, den, den_in, inv = mem.sb("inter", [P, 4, DV]), mem.sb("den", [P, 4]), mem.sb("den_in", [P, 4]), mem.sb("inv", [P, 4])
        square, mean = mem.sb("square", [P, 2, 4, DV]), mem.sb("mean", [P, 4])
        z_abs, z_log, la = mem.sb("z_abs", [P, 256]), mem.sb("z_log", [P, 256]), mem.sb("la", [P, 256])
        grow, shrink, to_end = mem.sb("grow", [P, 2, P]), mem.sb("shrink", [P, 2, P]), mem.sb("to_end", [P, 2, P])
        g_end, g_exp = mem.sb("g_end", [P, 2, 2]), mem.sb("g_exp", [P, 2, 2])
        k_inv, k_end = mem.sb("k_inv", [P, 2, P]), mem.sb("k_end", [P, 2, P])
        k_split, q_split = mem.sb("k_split", [P, 2, 2, P]), mem.sb("q_split", [P, 2, 2, P])
        q_chunk = mem.sb("q_chunk", [P, 2, 2, P])
        k_end_rows = mem.sb("k_end_rows", [P, 2, 256])
        att = mem.sb("att", [P, 4, P])
        A_, B_, C_, E_, G1, G2, G3, G4 = bank
        names = ("copied", "z_ready", "scores_ready", "inter_ready", "decay_sums", "p_turned", "update_ready", "att_ready",
                 "k_end_turned", "intra_ready", "outer_ready", "gla_ready", "weights_ready", "z_logged", "exps_ready", "p_copied",
                 "k_end_copied", "prob_ready", "k_rows_ready", "inter_taken", "la_ready", "state_ready", "gla_qk_ready",
                 "att_masked", "s_odd_ready", "dve_tile", "cleared")
        s = {n: mem.sem(n) for n in names}
        with nc.Block() as block:

            @block.gpsimd
            def _(pool):
                for t in (state, norm_state, s_even, s_odd, q_chunk, q_split, k_split, att, k_end_rows):
                    nc.gpsimd.memset(t[:], 0.0)
                pool.drain()
                pool.sem_inc(s["cleared"], 1)
                with pool.Fori(0, 8) as tile:
                    pool.wait_ge(s["dve_tile"], tile)
                    nc.gpsimd.tensor_copy(lr_t[:], lowrank[:, ds(P * tile, P)]).then_inc(s["copied"], 1)
                    pool.drain()
                    nc.gpsimd.tensor_copy(qk_t[:], qk[:, :, ds(P * tile, P)])
                    pool.drain()
                    nc.gpsimd.tensor_copy(k_split[0:DK, :, 0], qk[0:DK, 2:4, ds(P * tile, P)])
                    pool.drain()
                    nc.gpsimd.tensor_copy(k_split[DK:P, :, 1], qk[DK:P, 2:4, ds(P * tile, P)])
                    pool.drain()
                    pool.sem_inc(s["copied"], 1)

            @block.tensor
            def _(pe):
                with pe.Fori(0, 8) as tile:
                    n = tile + 1
                    pe.wait_ge(s["copied"], 2 * tile + 1)
                    nc.tensor.matmul(G1[:, 0:256], lr_t[:], c["lr_up"][:], start=True, stop=True).then_inc(s["z_ready"], 1)
                    pe.wait_ge(s["copied"], 2 * tile + 2)
                    for pair in range(2):
                        last = nc.tensor.matmul(A_[:, pair * 256:(pair + 1) * 256], qk_t[:, pair], k_split[:, pair],
                                                start=True, stop=True)
                    last.then_inc(s["scores_ready"], 1)
                    for pair in range(2):
                        last = nc.tensor.transpose(C_[:, pair * P:(pair + 1) * P], qk_t[:, 2 + pair], c["ident"][:])
                    pe.wait_ge(s["cleared"], 1)
                    pe.wait_ge(s["state_ready"], tile)
                    for pair in range(2):
                        nc.tensor.matmul(E_[:, pair * 256:(pair + 1) * 256], qk_t[:, pair], state[:, pair], start=True, stop=True)
                        last = nc.tensor.matmul(C_[:, 256 + 2 * pair:258 + 2 * pair], qk_t[:, pair], norm_state[:, pair], start=True, stop=True)
                    last.then_inc(s["inter_ready"], 1)
                    pe.wait_ge(s["la_ready"], n)
                    for pair in range(2):
                        last = nc.tensor.matmul(G1[:, 256 + pair * P:256 + (pair + 1) * P], la[:, pair * P:(pair + 1) * P], c["tri_gla"][:],
                                                start=True, stop=True)
                    last.then_inc(s["decay_sums"], 1)
                    pe.wait_ge(s["prob_ready"], n)
                    for h in range(4):
                        last = nc.tensor.transpose(A_[:, h * P:(h + 1) * P], prob[:, h], c["ident"][:])
                    last.then_inc(s["p_turned"], 1)
                    pe.wait_ge(s["k_rows_ready"], n)
                    pe.wait_ge(s["inter_taken"], n)
                    for pair in range(2):
                        k_pair = k_rows[:, 2 * pair:2 * pair + 2].rearrange("p h d -> p (h d)")
                        nc.tensor.matmul(E_[:, pair * 256:(pair + 1) * 256], k_pair, values[:, 0, tile, pair * 256:(pair + 1) * 256],
                                         start=True, stop=True)
                        last = nc.tensor.matmul(C_[:, 260 + pair:261 + pair], k_pair, c["ones"][:, 0:1], start=True, stop=True)
                    last.then_inc(s["update_ready"], 1)
                    pe.wait_ge(s["gla_qk_ready"], n)
                    for pair in range(2):
                        last = nc.tensor.matmul(G2[:, pair * 256:(pair + 1) * 256], k_inv[:, pair], q_split[:, pair], start=True, stop=True)
                    last.then_inc(s["att_ready"], 1)
                    for pair in range(2):
                        last = nc.tensor.transpose(G3[:, pair * P:(pair + 1) * P], k_end[:, pair], c["ident"][:])
                    last.then_inc(s["k_end_turned"], 1)
                    pe.wait_ge(s["p_copied"], n)
                    for h in range(4):
                        last = nc.tensor.matmul(B_[:, h * P:(h + 1) * P], prob_t[:, h], values[:, 0, tile, h * P:(h + 1) * P], start=True, stop=True)
                    last.then_inc(s["intra_ready"], 1)
                    pe.wait_ge(s["k_end_copied"], n)
                    for chunk, dst in ((0, G1), (1, G3)):
                        for pair in range(2):
                            last = nc.tensor.matmul(dst[:, pair * 256:(pair + 1) * 256], k_end_rows[:, chunk, pair * P:(pair + 1) * P],
                                                    values[:, 1, tile, pair * 256:(pair + 1) * 256], start=True, stop=True)
                    last.then_inc(s["outer_ready"], 1)
                    pe.wait_ge(s["s_odd_ready"], n)
                    for pair in range(2):
                        cols = slice(pair * 256, (pair + 1) * 256)
                        nc.tensor.matmul(G4[:, cols], q_chunk[:, 0, pair], s_even[:, pair], start=(pair == 0), stop=False,
                                         skip_group_check=True)
                        nc.tensor.matmul(G4[:, cols], q_chunk[:, 1, pair], s_odd[:, pair], start=False, stop=False, skip_group_check=True)
                        if pair == 0:
                            pe.wait_ge(s["att_masked"], n)
                        for h in (2 * pair, 2 * pair + 1):
                            last = nc.tensor.matmul(G4[:, h * P:(h + 1) * P], att[:, h], values[:, 1, tile, h * P:(h + 1) * P],
                                                    start=False, stop=(h == 3), skip_group_check=True)
                    last.then_inc(s["gla_ready"], 1)

            @block.scalar
            def _(act):
                with act.Fori(0, 8) as tile:
                    n = tile + 1
                    act.wait_ge(s["cleared"], 1)
                    act.wait_ge(s["dve_tile"], tile)
                    for h in range(4):
                        last = nc.scalar.activation(weight[:, h], shifted[:, tile, h], ACT.Exp, bias=neg_m[:, tile, h:h + 1])
                    last.then_inc(s["weights_ready"], 1)
                    act.wait_ge(s["z_ready"], n)
                    nc.scalar.activation(z_abs[:], G1[:, 0:256], ACT.Abs)
                    act.drain()
                    nc.scalar.activation(z_abs[:], z_abs[:], ACT.Exp, scale=-1.0)
                    act.drain()
                    nc.scalar.activation(z_log[:], z_abs[:], ACT.Ln, bias=1.0).then_inc(s["z_logged"], 1)
                    act.wait_ge(s["decay_sums"], n)
                    sums = G1[:, 256:512].rearrange("p (a c t) -> p a c t", a=2, c=2)
                    nc.scalar.activation(g_end[:], sums[:, :, :, GLA_CHUNK - 1], ACT.Copy)
                    nc.scalar.activation(grow[:].rearrange("p a t -> p (a t)"), G1[:, 256:512], ACT.Exp)
                    nc.scalar.activation(shrink[:].rearrange("p a t -> p (a t)"), G1[:, 256:512], ACT.Exp, scale=-1.0)
                    act.drain()
                    nc.scalar.activation(g_exp[:], g_end[:], ACT.Exp)
                    for pair in range(2):
                        for chunk in range(2):
                            last = nc.scalar.activation(to_end[:, pair, chunk * GLA_CHUNK:(chunk + 1) * GLA_CHUNK], sums[:, pair, chunk],
                                                        ACT.Exp, scale=-1.0, bias=g_end[:, pair, chunk:chunk + 1])
                    last.then_inc(s["exps_ready"], 1)
                    act.wait_ge(s["p_turned"], n)
                    nc.scalar.activation(prob_t[:].rearrange("p h t -> p (h t)"), A_[:], ACT.Copy).then_inc(s["p_copied"], 1)
                    act.wait_ge(s["k_end_turned"], n)
                    for chunk in range(2):
                        rows = slice(chunk * GLA_CHUNK, (chunk + 1) * GLA_CHUNK)
                        last = nc.scalar.activation(k_end_rows[rows, chunk], G3[rows, 0:256], ACT.Copy)
                    last.then_inc(s["k_end_copied"], 1)

            def per_head_blocks(dst, old, scale, update):
                for h in range(4):
                    lo, pair, half = DK * (h % 2), h // 2, h % 2
                    rows, cols = slice(lo, lo + DK), slice(half * DV, (half + 1) * DV)
                    last = nc.vector.scalar_tensor_tensor(dst[rows, pair, cols], old[rows, pair, cols], scale(rows, h),
                                                          update[rows, pair * 256 + half * DV:pair * 256 + (half + 1) * DV],
                                                          ALU.mult, ALU.add)
                return last

            @block.vector
            def _(dve):
                dve.wait_ge(s["cleared"], 1)
                with dve.Fori(0, 8) as tile:
                    n = tile + 1
                    dve.wait_ge(s["weights_ready"], n)
                    dve.wait_ge(s["scores_ready"], n)
                    nc.vector.scalar_tensor_tensor(prob[:].rearrange("p h t -> p (h t)"), A_[:], DK ** -0.5,
                                                   weight[:].rearrange("p h t -> p (h t)"), ALU.mult, ALU.mult).then_inc(s["prob_ready"], 1)
                    dve.wait_ge(s["inter_ready"], n)
                    nc.vector.scalar_tensor_tensor(k_rows[:], C_[:, 0:256].rearrange("p (h d) -> p h d", h=4), DK ** -0.5,
                                                   bc(k_weight[:, tile], 2, DK), ALU.mult, ALU.mult).then_inc(s["k_rows_ready"], 1)
                    dve.wait_ge(s["z_logged"], n)
                    nc.vector.scalar_tensor_tensor(la[:], G1[:, 0:256], 0.0, z_log[:], ALU.min, ALU.subtract).then_inc(s["la_ready"], 1)
                    dve.drain()
                    nc.vector.tensor_tensor(inter[:], E_[:].rearrange("p (h d) -> p h d", h=4), bc(s_inter[:, tile], 2, DV), ALU.mult)
                    nc.vector.tensor_tensor(den[:], C_[:, 256:260], s_inter[:, tile], ALU.mult)
                    nc.vector.tensor_reduce(den_in[:], prob[:], AX.X, ALU.add)
                    dve.drain()
                    dve.sem_inc(s["inter_taken"], 1)
                    nc.vector.tensor_tensor(den[:], den[:], den_in[:], ALU.add)
                    dve.drain()
                    nc.vector.scalar_tensor_tensor(den_in[:], den[:], -1.0, den[:], ALU.mult, ALU.max)
                    dve.drain()
                    nc.vector.tensor_tensor(den[:], den_in[:], floor[:, tile], ALU.max)
                    dve.drain()
                    nc.vector.reciprocal(inv[:], den[:])
                    dve.wait_ge(s["exps_ready"], n)
                    gk = gqk[:, 2:4, ds(P * tile, P)]
                    for half in range(2):
                        rows = slice(DK * half, DK * half + DK)
                        nc.vector.tensor_tensor(q_split[rows, :, half], gqk[rows, 0:2, ds(P * tile, P)], grow[rows], ALU.mult)
                    nc.vector.scalar_tensor_tensor(k_inv[:], gk, DK ** -0.5, shrink[:], ALU.mult, ALU.mult)
                    nc.vector.scalar_tensor_tensor(k_end[:], gk, DK ** -0.5, to_end[:], ALU.mult, ALU.mult)
                    for chunk in range(2):
                        span = slice(chunk * GLA_CHUNK, (chunk + 1) * GLA_CHUNK)
                        nc.vector.tensor_tensor(q_chunk[:, chunk, :, span], gqk[:, 0:2, ds(P * tile + GLA_CHUNK * chunk, GLA_CHUNK)],
                                                grow[:, :, span], ALU.mult)
                    dve.drain()
                    dve.sem_inc(s["gla_qk_ready"], 1)
                    dve.wait_ge(s["att_ready"], n)
                    dve.wait_ge(s["update_ready"], n)
                    per_head_blocks(state, state, lambda rows, h: decay[rows, tile, h:h + 1], E_)
                    for h in range(4):
                        rows, pair, half = slice(DK * (h % 2), DK * (h % 2) + DK), h // 2, h % 2
                        cell = norm_state[rows, pair, half:half + 1]
                        nc.vector.scalar_tensor_tensor(cell, cell, decay[rows, tile, h:h + 1], C_[rows, 260 + pair:261 + pair], ALU.mult, ALU.add)
                    dve.drain()
                    dve.sem_inc(s["state_ready"], 1)
                    nc.vector.copy_predicated(att[:], bc(c["gla_mask"][:].bitcast(I32), 1, 4), G2[:].rearrange("p (h t) -> p h t", h=4))\
                        .then_inc(s["att_masked"], 1)
                    dve.wait_ge(s["intra_ready"], n)
                    nc.vector.tensor_tensor(inter[:], inter[:], B_[:].rearrange("p (h d) -> p h d", h=4), ALU.add)
                    dve.drain()
                    nc.vector.tensor_tensor(inter[:], inter[:], bc(inv[:], 2, DV), ALU.mult)
                    dve.drain()
                    nc.vector.tensor_reduce(mean[:], inter[:], AX.X, ALU.add)
                    dve.wait_ge(s["outer_ready"], n)
                    per_head_blocks(s_odd, s_even, lambda rows, h: g_exp[rows, h // 2, 0:1], G1)
                    dve.drain()
                    dve.sem_inc(s["s_odd_ready"], 1)
                    ml_out = hidden[:, 0, tile].rearrange("p (h d) -> p h d", h=4)
                    nc.vector.scalar_tensor_tensor(ml_out, bc(mean[:], 2, DV), -1.0 / DV, inter[:], ALU.mult, ALU.add)
                    dve.wait_ge(s["gla_ready"], n)
                    per_head_blocks(s_even, s_odd, lambda rows, h: g_exp[rows, h // 2, 1:2], G3)
                    gla_out = hidden[:, 1, tile].rearrange("p (h d) -> p h d", h=4)
                    nc.vector.tensor_copy(gla_out, G4[:].rearrange("p (h d) -> p h d", h=4))
                    dve.drain()
                    both = hidden[:, :, tile].rearrange("p m (h d) -> p m h d", h=4)
                    nc.vector.tensor_tensor(square[:], both, both, ALU.mult)
                    dve.drain()
                    nc.vector.tensor_reduce(spread[:, :, tile], square[:], AX.X, ALU.add)
                    dve.drain()
                    dve.sem_inc(s["dve_tile"], 1)


def layer0(nc, base, c, A, h):
    with ExitStack() as ctx:
        mem = Memory(nc, ctx, "l0")
        scale = mem.sb("scale", [P, 8])
        hidden_gates = mem.sb("gates", [P, 2, 8, BANK])
        spread = mem.sb("spread", [P, 2, 8, 4])
        with ExitStack() as inner:
            tmp = Memory(nc, inner, "l0t")
            qk, gqk = tmp.sb("qk", [P, 4, CONV_K - 1 + 1024]), tmp.sb("gqk", [P, 4, 1024])
            values = tmp.sb("values", [P, 2, 8, BANK])
            if_rows, lowrank = tmp.sb("if_rows", [P, 8, 8]), tmp.sb("lowrank", [LOWRANK + 1, 1024])
            with ExitStack() as first:
                uT = Memory(nc, first, "l0u").sb("uT", [P, 8, 8, P])
                row_scales(nc, "l0scale", c, h, scale)
                layer0_inputs(nc, c, A, h, uT, scale)
                layer0_projection(nc, c, A, uT, qk, gqk, values, hidden_gates, if_rows, lowrank)
            hidden = values
            layer0_mixers(nc, c, qk, gqk, values, if_rows, lowrank, hidden, spread)
            with ExitStack() as last_ctx:
                m2 = Memory(nc, last_ctx, "l0n")
                inv = m2.sb("inv", [P, 2, 8, 4])
                rooted = m2.sem("rooted")
                with nc.Block() as block:

                    @block.scalar
                    def _(act):
                        nc.scalar.activation(inv[:], spread[:], ACT.Sqrt, bias=c["eps"][:], scale=1.0 / DV).then_inc(rooted, 1)

                    @block.vector
                    def _(dve):
                        dve.wait_ge(rooted, 1)
                        nc.vector.reciprocal(inv[:], inv[:])
                        dve.drain()
                        for mixer in range(2):
                            x = hidden[:, mixer].rearrange("p t (h d) -> p (t h) d", h=4)
                            nc.vector.tensor_tensor(x, x, bc(inv[:, mixer].rearrange("p t h -> p (t h)"), 2, DV), ALU.mult)
                            dve.drain()
                            nc.vector.tensor_tensor(hidden_gates[:, mixer], hidden_gates[:, mixer], hidden[:, mixer], ALU.mult)
        with ExitStack() as out_ctx:
            m3 = Memory(nc, out_ctx, "l0o")
            w_out = m3.sb("w_out", [P, 8, 1024])
            w_ready = m3.sem("w_ready")
            with nc.Block() as block:

                @block.sync
                def _(sp):
                    sp.dma_start(w_out[:], A["ab_w_out"][0].rearrange("(k p) n -> p k n", p=P)).then_inc(w_ready, 16)

            def rows_of(act, tile, slot):
                return nc.scalar.activation(slot.rearrange("p (m n) -> p m n", m=2), hidden_gates[:, :, tile], ACT.Copy)

            def take(dve, tile, bank):
                return nc.vector.tensor_tensor(h[:, tile], h[:, tile], bank[:], ALU.add)

            project_tiles(nc, "l0out", c, rows_of, c["y_gain"], w_out, 1024, take, weights_ready=(w_ready, 16))


N_BLOCKS = N_EXPERTS + (1024 * TOP_K) // P
UNUSED = 4096


def route(nc, c, layer, logits, weight, rows_u, rows_y, over):
    with ExitStack() as ctx:
        mem = Memory(nc, ctx, f"route{layer}")
        t8 = lambda name, *shape: mem.sb(name, [P, 8, *shape])
        g_top, g_sum, g_idx, g_shift = t8("g_top"), t8("g_sum"), t8("g_idx"), t8("g_shift", 4)
        g_hot, by_group, chosen, flags = t8("g_hot", 4), t8("by_group", 4, 8), t8("chosen", 8), t8("flags", 8)
        top = mem.sb("top", [P, 2, 8])
        idx = mem.sb("idx", [P, 2, 8])
        hot = mem.sb("hot", [P, 2, 8, N_EXPERTS])
        both, before = t8("both", N_EXPERTS), t8("before", N_EXPERTS)
        pos_all, work = t8("pos_all", N_EXPERTS), mem.sb("work", [P, 2, 8, N_EXPERTS])
        count, extra, start, start2, end = (mem.sb(x, [P, N_EXPERTS]) for x in ("count", "extra", "start", "start2", "end"))
        count_i = mem.sb("count_i", [P, N_EXPERTS], I32)
        pos, slot, nth, first, column, is_first = (mem.sb(x, [P, 2, 8]) for x in ("pos", "slot", "nth", "first", "column", "is_first"))
        pos_i, part_i = mem.sb("pos_i", [P, 2, 8], I32), mem.sb("part_i", [P, 2, 8], I32)
        value = mem.sb("value", [P, 2, 8])
        slot_hot = mem.sb("slot_hot", [P, 16, P])
        block_hot = mem.sb("block_hot", [P, 16, N_BLOCKS])
        table, none = mem.sb("table", [P, N_BLOCKS]), mem.sb("none", [P, N_BLOCKS])
        owner, owner2 = mem.sb("owner", [P, 16, N_EXPERTS]), mem.sb("owner2", [P, 16, N_EXPERTS])
        over_f = mem.sb("over_f", [P, 17])
        ranks, counts, made = mem.ps("ranks", [P, 8, N_EXPERTS]), mem.ps("counts", [P, N_EXPERTS]), mem.ps("made", [P, N_BLOCKS])
        shifted, powered, hot_ready, ranked, tabled, tables_ready = (
            mem.sem(x) for x in ("shifted", "powered", "hot_ready", "ranked", "tabled", "tables_ready"))
        iota = c["iota"]
        FAR = 99.0
        with nc.Block() as block:

            @block.scalar
            def _(act):
                act.wait_ge(shifted, 1)
                nc.scalar.activation(g_shift[:], g_shift[:], ACT.Exp).then_inc(powered, 1)
                act.wait_ge(shifted, 2)
                nc.scalar.activation(top[:, 1], top[:, 1], ACT.Exp).then_inc(powered, 1)

            @block.tensor
            def _(pe):
                pe.wait_ge(hot_ready, 1)
                flat = lambda x: x.rearrange("p t e -> p (t e)")
                nc.tensor.matmul(flat(ranks[:]), c["tri_strict"][:], flat(both[:]), start=True, stop=False)
                nc.tensor.matmul(flat(ranks[:]), c["ones"][:], flat(before[:]), start=False, stop=True)
                nc.tensor.matmul(counts[:], c["ones"][:], both[:, 7], start=True, stop=False)
                nc.tensor.matmul(counts[:], c["ones"][:], before[:, 7], start=False, stop=True).then_inc(ranked, 1)
                pe.wait_ge(tables_ready, 1)
                for n in range(16):
                    last = nc.tensor.matmul(made[:], slot_hot[:, n], block_hot[:, n], start=(n == 0), stop=(n == 15))
                last.then_inc(tabled, 1)

            @block.vector
            def _(dve):
                v = nc.vector

                def first_of(dst, values, best, n, scratch):
                    v.tensor_tensor(scratch[:], values, bc(best, 2, n), ALU.is_ge)
                    dve.drain()
                    v.scalar_tensor_tensor(scratch[:], bc(iota[:, 0:n], 1, 8), -FAR, scratch[:], ALU.add, ALU.mult)
                    dve.drain()
                    v.tensor_reduce(dst, scratch[:], AX.X, ALU.min)
                    dve.drain()
                    v.tensor_scalar(dst, dst, FAR, None, ALU.add)
                    dve.drain()

                g_logits = logits[:, :, 0:4]
                v.tensor_reduce(g_top[:], g_logits, AX.X, ALU.max)
                dve.drain()
                v.tensor_tensor(g_shift[:], g_logits, bc(g_top[:], 2, 4), ALU.subtract).then_inc(shifted, 1)
                first_of(g_idx[:], g_logits, g_top[:], 4, g_hot)
                v.tensor_tensor(g_hot[:], bc(iota[:, 0:4], 1, 8), bc(g_idx[:], 2, 4), ALU.is_equal)
                dve.drain()
                v.tensor_tensor(by_group[:], logits[:, :, 4:36].rearrange("p t (g e) -> p t g e", g=4), bc(g_hot[:], 3, 8), ALU.mult)
                dve.drain()
                v.tensor_reduce(chosen[:], by_group[:].rearrange("p t g e -> p t e g"), AX.X, ALU.add)
                dve.drain()
                v.tensor_reduce(top[:, 0], chosen[:], AX.X, ALU.max)
                dve.drain()
                first_of(idx[:, 0], chosen[:], top[:, 0], 8, flags)
                v.tensor_tensor(flags[:], bc(iota[:, 0:8], 1, 8), bc(idx[:, 0], 2, 8), ALU.is_equal)
                dve.drain()
                v.scalar_tensor_tensor(chosen[:], flags[:], NEG, chosen[:], ALU.mult, ALU.add)
                dve.drain()
                v.tensor_reduce(top[:, 1], chosen[:], AX.X, ALU.max)
                dve.drain()
                first_of(idx[:, 1], chosen[:], top[:, 1], 8, flags)
                v.tensor_tensor(top[:, 1], top[:, 1], top[:, 0], ALU.subtract).then_inc(shifted, 1)
                dve.wait_ge(powered, 1)
                v.tensor_reduce(g_sum[:], g_shift[:], AX.X, ALU.add)
                dve.wait_ge(powered, 2)
                v.tensor_scalar(top[:, 0], top[:, 1], 1.0, None, ALU.add)
                dve.drain()
                v.tensor_tensor(top[:, 0], top[:, 0], g_sum[:], ALU.mult)
                dve.drain()
                v.reciprocal(weight[:, 0], top[:, 0])
                dve.drain()
                v.tensor_tensor(weight[:, 1], weight[:, 0], top[:, 1], ALU.mult)
                for k in range(2):
                    v.scalar_tensor_tensor(idx[:, k], g_idx[:], float(PER_GROUP), idx[:, k], ALU.mult, ALU.add)
                dve.drain()
                for k in range(2):
                    v.tensor_tensor(hot[:, k], bc(iota[:, 0:N_EXPERTS], 1, 8), bc(idx[:, k], 2, N_EXPERTS), ALU.is_equal)
                dve.drain()
                v.tensor_tensor(both[:], hot[:, 0], hot[:, 1], ALU.add)
                v.memset(before[:, 0], 0.0)
                dve.drain()
                for tile in range(1, 8):
                    last = v.tensor_tensor(before[:, tile], before[:, tile - 1], both[:, tile - 1], ALU.add)
                    dve.drain()
                dve.sem_inc(hot_ready, 1)
                dve.wait_ge(ranked, 1)
                v.tensor_copy(pos_all[:], ranks[:])
                v.tensor_scalar(count_i[:], counts[:], float(P - 1), None, ALU.add)
                dve.drain()
                v.tensor_scalar(count_i[:], count_i[:], 7, None, ALU.logical_shift_right)
                dve.drain()
                v.tensor_copy(extra[:], count_i[:])
                dve.drain()
                v.tensor_scalar(extra[:], extra[:], -1.0, 0.0, ALU.add, ALU.max)
                dve.drain()
                v.tensor_copy(end[:], extra[:])
                dve.drain()
                a, b = end, start2
                for step in (1, 2, 4, 8, 16):
                    v.tensor_copy(b[:, 0:step], a[:, 0:step])
                    v.tensor_tensor(b[:, step:], a[:, step:], a[:, 0:N_EXPERTS - step], ALU.add)
                    dve.drain()
                    a, b = b, a
                total = a
                v.tensor_tensor(start[:], total[:], extra[:], ALU.subtract)
                dve.drain()
                for k in range(2):
                    v.tensor_tensor(work[:, k], hot[:, k], pos_all[:], ALU.mult)
                dve.drain()
                v.tensor_reduce(pos[:], work[:], AX.X, ALU.add)
                dve.drain()
                for k in range(2):
                    v.tensor_tensor(work[:, k], hot[:, k], bc(start[:], 1, 8), ALU.mult)
                v.tensor_copy(pos_i[:], pos[:])
                dve.drain()
                v.tensor_reduce(first[:], work[:], AX.X, ALU.add)
                v.tensor_scalar(part_i[:], pos_i[:], P - 1, None, ALU.bitwise_and)
                v.tensor_scalar(pos_i[:], pos_i[:], 7, None, ALU.logical_shift_right)
                dve.drain()
                v.tensor_copy(slot[:], part_i[:])
                v.tensor_copy(nth[:], pos_i[:])
                dve.drain()
                v.tensor_scalar(is_first[:], nth[:], 0.0, None, ALU.is_equal)
                v.tensor_tensor(column[:], first[:], nth[:], ALU.add)
                dve.drain()
                v.tensor_scalar(column[:], column[:], float(N_EXPERTS - 1), None, ALU.add)
                dve.drain()
                v.tensor_tensor(idx[:], idx[:], column[:], ALU.subtract)
                dve.drain()
                v.tensor_tensor(idx[:], idx[:], is_first[:], ALU.mult)
                dve.drain()
                v.tensor_tensor(column[:], column[:], idx[:], ALU.add)
                for k in range(2):
                    v.tensor_scalar(value[:, k], c["token2"][:], float(1 + k), None, ALU.add)
                dve.drain()
                flat = lambda x: x[:].rearrange("p k t -> p (k t)")
                v.tensor_tensor(slot_hot[:], bc(iota[:], 1, 16), bc(flat(slot), 2, P), ALU.is_equal)
                v.tensor_tensor(block_hot[:], bc(iota[:, 0:N_BLOCKS], 1, 16), bc(flat(column), 2, N_BLOCKS), ALU.is_equal)
                dve.drain()
                v.tensor_tensor(block_hot[:], block_hot[:], bc(flat(value), 2, N_BLOCKS), ALU.mult)
                dve.drain()
                dve.sem_inc(tables_ready, 1)
                v.tensor_tensor(owner[:], bc(iota[:, 0:16], 2, N_EXPERTS), bc(total[:], 1, 16), ALU.is_ge)
                v.tensor_copy(over_f[:, 0:1], total[:, N_EXPERTS - 1:N_EXPERTS])
                dve.drain()
                v.tensor_reduce(over_f[:, 1:17], owner[:], AX.X, ALU.add)
                dve.drain()
                v.tensor_scalar(over_f[:, 1:17], over_f[:, 1:17], float(N_EXPERTS - 1), None, ALU.min)
                dve.drain()
                v.tensor_copy(over[:], over_f[0:1, :])
                dve.wait_ge(tabled, 1)
                v.tensor_scalar(none[:], made[:], 0.0, float(UNUSED + 1), ALU.is_equal, ALU.mult)
                dve.drain()
                v.scalar_tensor_tensor(table[:], made[:], -1.0, none[:], ALU.add, ALU.add)
                dve.drain()
                v.tensor_copy(rows_y[:], table[:])
                dve.drain()
                v.tensor_scalar(rows_u[:], rows_y[:], 1, None, ALU.logical_shift_right)


def split_tensor(mem, name, shape):
    return mem.sb(f"{name}_hi", shape, F32R), mem.sb(f"{name}_lo", shape, F32R)


def experts(nc, c, A, layer, gain, u_rows, y_rows, rows_u, rows_y, raw, raw_ready):
    E, UNITS, RAW, SPLIT = N_EXPERTS, 12, len(raw), 4
    last_pair = E // 2 - 1
    halves = lambda name: A[name][layer].rearrange("e (a k p) n -> e a p k n", p=P, a=2)
    w_gate, w_up, w_down = halves("expert_w_gate"), halves("expert_w_up"), halves("expert_w_down")
    with ExitStack() as ctx:
        mem = Memory(nc, ctx, f"exp{layer}")
        two = lambda name, shape, dt=F32: [mem.sb(f"{name}{j}", shape, dt) for j in range(2)]
        split = [split_tensor(mem, f"w{s}", [P, 2048]) for s in range(SPLIT)]
        x_rows, x_scaled = two("x_rows", [P, 1024]), mem.sb("x_scaled", [P, 8, P])
        x_hi, x_lo = split_tensor(mem, "x", [P, 8, P])
        hid_hi, hid_lo = split_tensor(mem, "hid", [P, 4, P])
        silu, hid, y = mem.sb("silu", [P, BANK]), mem.sb("hid", [P, BANK]), two("y", [P, 1024])
        idx_u, idx_y = two("idx_u", [P, 1], I32), two("idx_y", [P, 1], I32)
        x_turned = mem.ps("x_turned", [P, 8, P])
        gate_out, up_out = mem.ps("gate_out", [P, BANK]), mem.ps("up_out", [P, BANK])
        hid_turned, y_out = mem.ps("hid_turned", [P, 4, P]), mem.ps("y_out", [P, 1024])
        gathered, scattered = ([mem.sem(f"{name}{j}") for j in range(2)] for name in ("gathered", "scattered"))
        lo_ready = [mem.sem(f"lo_ready{s}") for s in range(SPLIT)]
        hi_ready, unit_done, x_turned_s, x_scaled_s, x_hi_s, x_cols_s, silu_done, hid_ready, hid_turned_s, hid_hi_s, hid_cols_s, y_copied, y_free = (
            mem.sem(x) for x in ("hi_ready", "unit_done", "x_turned", "x_scaled", "x_hi", "x_cols", "silu_done", "hid_ready",
                                 "hid_turned", "hid_hi", "hid_cols", "y_copied", "y_free"))

        number = lambda unit: unit[0] * UNITS + (4 + unit[1])
        raw_slot = lambda unit: (4 + unit[1]) % RAW
        split_slot = lambda unit: (4 + unit[1]) % SPLIT
        loaded_count = lambda unit: (unit[0] * (UNITS // RAW) + (4 + unit[1]) // RAW + 1) * 16
        lo_count = lambda unit: unit[0] * (UNITS // SPLIT) + (4 + unit[1]) // SPLIT + 2
        done_count = lambda unit: number(unit) + 1 + SPLIT

        with nc.Block() as block:

            @block.sync
            def _(sp):
                def load(unit, src):
                    s = raw_slot(unit)
                    sp.wait_ge(lo_ready[split_slot((0, unit[1] - RAW))], lo_count((unit[0], unit[1] - RAW)))
                    dst = raw[s][:].rearrange("p (k n) -> p k n", k=src.shape[1])
                    sp.dma_start(dst, src).then_inc(raw_ready[s], 16)

                def gate_of(e, pair, u):
                    for half in range(2):
                        load((pair, u + half), w_gate[e, half])

                def up_then_down(e, pair, u):
                    for half in range(2):
                        load((pair, u + half), w_up[e, half])
                    for half in range(2):
                        load((pair, u + 2 + half), w_down[e - 1, half])

                with sp.Fori(0, last_pair) as pair:
                    for q in range(2):
                        e = 2 * pair + 1 + q
                        up_then_down(e, pair, 6 * q + 2)
                        gate_of(e + 1, pair, 6 * q + 6)
                up_then_down(E - 1, last_pair, 2)
                for half in range(2):
                    load((last_pair, 6 + half), w_down[E - 1, half])

            def make_lo(engine, vec, unit):
                engine.wait_ge(hi_ready, number(unit) + 1)
                hi, lo = split[split_slot(unit)]
                vec.tensor_tensor(lo[:], raw[raw_slot(unit)][:], hi[:].bitcast(F32), ALU.subtract).then_inc(lo_ready[split_slot(unit)], 1)

            @block.gpsimd
            def _(pool):
                for j in range(2):
                    nc.gpsimd.memset(x_rows[j][:], 0.0)
                pool.sem_inc(y_free, 2)
                pool.drain()

                def scatter(e, j):
                    pool.wait_ge(y_copied, e + 2)
                    nc.gpsimd.tensor_copy(idx_y[j][:], rows_y[:, ds(e, 1)])
                    pool.drain()
                    pool.indirect_dma_start(y_rows, bass.IndirectOffsetOnAxis(ap=idx_y[j][:], axis=0), y[j][:], None,
                                            bounds_check=2047, oob_is_err=False).then_inc(scattered[j], 16)

                def finish(j, pair):
                    pool.wait_ge(scattered[j], 16 * pair + 16)
                    pool.sem_inc(y_free, 1)

                def gather(e, j):
                    nc.gpsimd.tensor_copy(idx_u[j][:], rows_u[:, ds(e, 1)])
                    pool.drain()
                    pool.indirect_dma_start(x_rows[j][:], None, u_rows, bass.IndirectOffsetOnAxis(ap=idx_u[j][:], axis=0),
                                            bounds_check=1023, oob_is_err=False).then_inc(gathered[j], 16)

                gather(0, 0)
                gather(1, 1)
                for e in (2, 3):
                    pool.wait_ge(x_turned_s, e - 1)
                    gather(e, e % 2)
                make_lo(pool, nc.gpsimd, (0, 8))
                with pool.Fori(0, last_pair - 1) as pair:
                    for q in range(2):
                        e = 2 * pair + 1 + q
                        scatter(e - 1, q)
                        pool.wait_ge(x_turned_s, e + 2)
                        gather(e + 3, q)
                        make_lo(pool, nc.gpsimd, (pair, 6 * q + 14))
                        finish(q, pair)
                scatter(E - 4, 0)
                make_lo(pool, nc.gpsimd, (last_pair - 1, 14))
                finish(0, last_pair - 1)
                scatter(E - 3, 1)
                finish(1, last_pair - 1)
                scatter(E - 2, 0)
                scatter(E - 1, 1)
                finish(0, last_pair)
                finish(1, last_pair)

            @block.tensor
            def _(pe):
                pe.sem_inc(unit_done, SPLIT)
                pe.sem_inc(hid_turned_s, 1)

                def turn_x(e, j, pair):
                    pe.wait_ge(gathered[j], 16 * pair + 16)
                    for k in range(8):
                        last = nc.tensor.transpose(x_turned[:, k], x_rows[j][:, k * P:(k + 1) * P], c["ident"][:])
                    last.then_inc(x_turned_s, 1)

                def multiply(unit, x_parts, k0, K, outs, first, last_unit):
                    s = split_slot(unit)
                    pe.wait_ge(lo_ready[s], lo_count(unit))
                    w_hi, w_lo = (part[:].rearrange("p (k n) -> p k n", k=K) for part in split[s])
                    hi, lo = x_parts
                    for k in range(K):
                        for n, out in enumerate(outs):
                            cols = slice(n * BANK, (n + 1) * BANK)
                            for t, (x, w) in enumerate(((hi, w_hi), (hi, w_lo), (lo, w_hi))):
                                last = nc.tensor.matmul(out, x[:, k0 + k], w[:, k, cols], start=(first and k == 0 and t == 0),
                                                        stop=(last_unit and k == K - 1 and t == 2))
                    last.then_inc(unit_done, 1)

                def gate_up(e, unit):
                    pair, u = unit
                    pe.wait_ge(x_cols_s, e + 1)
                    pe.wait_ge(hid_ready, e + 1)
                    for m, out in enumerate((gate_out, up_out)):
                        for half in range(2):
                            multiply((pair, u + 2 * m + half), (x_hi, x_lo), 4 * half, 4, [out[:]], half == 0, half == 1)

                def down_of(e, unit):
                    pair, u = unit
                    pe.wait_ge(hid_cols_s, e + 1)
                    pe.wait_ge(y_copied, e + 1)
                    for half in range(2):
                        multiply((pair, u + half), (hid_hi, hid_lo), 2 * half, 2, [y_out[:, 0:BANK], y_out[:, BANK:]], half == 0, half == 1)

                def turn_hid(e):
                    pe.wait_ge(hid_ready, e + 2)
                    for k in range(4):
                        last = nc.tensor.transpose(hid_turned[:, k], hid[:, k * P:(k + 1) * P], c["ident"][:])
                    last.then_inc(hid_turned_s, 1)

                turn_x(0, 0, 0)
                gate_up(0, (-1, 8))
                turn_x(1, 1, 0)
                turn_hid(0)
                with pe.Fori(0, last_pair) as pair:
                    for q in range(2):
                        e = 2 * pair + 1 + q
                        gate_up(e, (pair, 6 * q))
                        turn_x(e + 1, q, pair + 1)
                        down_of(e - 1, (pair, 6 * q + 4))
                        turn_hid(e)
                gate_up(E - 1, (last_pair, 0))
                down_of(E - 2, (last_pair, 4))
                turn_hid(E - 1)
                down_of(E - 1, (last_pair, 6))

            @block.scalar
            def _(act):
                act.sem_inc(y_copied, 1)

                def make_hi(unit):
                    act.wait_ge(raw_ready[raw_slot(unit)], loaded_count(unit))
                    act.wait_ge(unit_done, number(unit) + 1)
                    nc.scalar.activation(split[split_slot(unit)][0][:], raw[raw_slot(unit)][:], ACT.Copy).then_inc(hi_ready, 1)

                def x_high(e):
                    act.wait_ge(x_scaled_s, e + 1)
                    nc.scalar.activation(x_hi[:], x_scaled[:], ACT.Copy).then_inc(x_hi_s, 1)

                def silu_of(e, gate_unit):
                    act.wait_ge(unit_done, done_count(gate_unit))
                    act.wait_ge(hid_ready, e + 1)
                    nc.scalar.activation(silu[:], gate_out[:], ACT.Silu).then_inc(silu_done, 1)

                def hid_high(e):
                    act.wait_ge(hid_turned_s, e + 2)
                    nc.scalar.activation(hid_hi[:], hid_turned[:], ACT.Copy).then_inc(hid_hi_s, 1)

                def copy_y(e, j, down_unit):
                    act.wait_ge(unit_done, done_count(down_unit))
                    act.wait_ge(y_free, e + 1)
                    nc.scalar.activation(y[j][:], y_out[:], ACT.Copy).then_inc(y_copied, 1)

                x_high(0)
                for u in range(8, 13):
                    make_hi((-1, u))
                silu_of(0, (-1, 9))
                for u in range(13, 15):
                    make_hi((-1, u))
                x_high(1)
                hid_high(0)
                with act.Fori(0, last_pair) as pair:
                    for q in range(2):
                        e, u = 2 * pair + 1 + q, 6 * q
                        make_hi((pair, u + 3))
                        make_hi((pair, u + 4))
                        silu_of(e, (pair, u + 1))
                        make_hi((pair, u + 5))
                        make_hi((pair, u + 6))
                        make_hi((pair, u + 7))
                        x_high(e + 1)
                        make_hi((pair, u + 8))
                        copy_y(e - 1, q, (pair, u + 5))
                        hid_high(e)
                make_hi((last_pair, 3))
                make_hi((last_pair, 4))
                silu_of(E - 1, (last_pair, 1))
                for u in range(5, 8):
                    make_hi((last_pair, u))
                copy_y(E - 2, 0, (last_pair, 5))
                hid_high(E - 1)
                copy_y(E - 1, 1, (last_pair, 7))

            @block.vector
            def _(dve):
                for s in range(SPLIT):
                    dve.sem_inc(lo_ready[s], 1)
                dve.sem_inc(hid_ready, 1)

                def x_columns(e):
                    dve.wait_ge(x_turned_s, e + 1)
                    for half in range(2):
                        last = nc.vector.tensor_tensor(x_scaled[:, 4 * half:4 * half + 4], x_turned[:, 4 * half:4 * half + 4],
                                                       bc(gain[:, 4 * half:4 * half + 4], 2, P), ALU.mult)
                    last.then_inc(x_scaled_s, 1)
                    dve.wait_ge(x_hi_s, e + 1)
                    nc.vector.tensor_tensor(x_lo[:], x_scaled[:], x_hi[:].bitcast(F32), ALU.subtract).then_inc(x_cols_s, 1)

                def silu_times_up(e, up_unit):
                    dve.wait_ge(unit_done, done_count(up_unit))
                    dve.wait_ge(silu_done, e + 1)
                    dve.wait_ge(hid_turned_s, e + 1)
                    nc.vector.tensor_tensor(hid[:], silu[:], up_out[:], ALU.mult).then_inc(hid_ready, 1)

                def hid_low(e):
                    dve.wait_ge(hid_hi_s, e + 1)
                    nc.vector.tensor_tensor(hid_lo[:], hid_turned[:], hid_hi[:].bitcast(F32), ALU.subtract).then_inc(hid_cols_s, 1)

                x_columns(0)
                for u in range(8, 15):
                    make_lo(dve, nc.vector, (-1, u))
                silu_times_up(0, (-1, 11))
                x_columns(1)
                hid_low(0)
                with dve.Fori(0, last_pair) as pair:
                    for q in range(2):
                        e, u = 2 * pair + 1 + q, 6 * q
                        for ahead in range(3, 7):
                            make_lo(dve, nc.vector, (pair, u + ahead))
                        silu_times_up(e, (pair, u + 3))
                        x_columns(e + 1)
                        make_lo(dve, nc.vector, (pair, u + 7))
                        hid_low(e)
                for u in range(3, 7):
                    make_lo(dve, nc.vector, (last_pair, u))
                silu_times_up(E - 1, (last_pair, 3))
                make_lo(dve, nc.vector, (last_pair, 7))
                hid_low(E - 1)


def experts_over(nc, c, A, layer, gain, u_rows, y_rows, rows_u, rows_y, over):
    w_gate = A["expert_w_gate"][layer].rearrange("e (k p) n -> e p k n", p=P)
    w_up = A["expert_w_up"][layer].rearrange("e (k p) n -> e p k n", p=P)
    w_down = A["expert_w_down"][layer].rearrange("e (k p) n -> e p k n", p=P)
    n_over = N_BLOCKS - N_EXPERTS
    with ExitStack() as ctx:
        mem = Memory(nc, ctx, f"over{layer}")
        gate, up, down = mem.sb("gate", [P, 8, BANK]), mem.sb("up", [P, 8, BANK]), mem.sb("down", [P, 4, 1024])
        x_rows, x_cols = mem.sb("x_rows", [P, 1024]), mem.sb("x_cols", [P, 8, P])
        silu, hid, hid_cols, y = mem.sb("silu", [P, BANK]), mem.sb("hid", [P, BANK]), mem.sb("hid_cols", [P, 4, P]), mem.sb("y", [P, 1024])
        idx_u, idx_y = mem.sb("idx_u", [P, 1], I32), mem.sb("idx_y", [P, 1], I32)
        x_turned, gate_out, up_out = mem.ps("x_turned", [P, 8, P]), mem.ps("gate_out", [P, BANK]), mem.ps("up_out", [P, BANK])
        hid_turned, y_out = mem.ps("hid_turned", [P, 4, P]), mem.ps("y_out", [P, 1024])
        names = ("weights", "gathered", "x_turned_", "x_cols_", "multiplied", "silued", "hid_", "hid_turned_", "hid_cols_", "y_made", "y_copied", "scattered", "stored")
        s = {n: mem.sem(n) for n in names}

        def each_block(engine, body):
            count = engine.value_load(over[0:1, 0:1], min_val=0, max_val=n_over)
            with engine.If(count > 0):
                with engine.Fori(0, n_over) as b:
                    with engine.If(count > b):
                        body(b)

        with nc.Block() as block:

            @block.sync
            def _(sp):
                def body(b):
                    owner = sp.value_load(over[0:1, ds(b + 1, 1)], min_val=0, max_val=N_EXPERTS - 1)
                    sp.wait_ge(s["y_made"], b)
                    for dst, src in ((gate, w_gate), (up, w_up), (down, w_down)):
                        sp.dma_start(dst[:], src[ds(owner, 1)].rearrange("e p k n -> p (e k) n")).then_inc(s["weights"], 16)
                each_block(sp, body)

            @block.gpsimd
            def _(pool):
                nc.gpsimd.memset(x_rows[:], 0.0)
                pool.drain()

                def body(b):
                    nc.gpsimd.tensor_copy(idx_u[:], rows_u[:, ds(b + N_EXPERTS, 1)])
                    pool.drain()
                    pool.indirect_dma_start(x_rows[:], None, u_rows, bass.IndirectOffsetOnAxis(ap=idx_u[:], axis=0),
                                            bounds_check=1023, oob_is_err=False).then_inc(s["gathered"], 16)
                    pool.wait_ge(s["y_copied"], b + 1)
                    nc.gpsimd.tensor_copy(idx_y[:], rows_y[:, ds(b + N_EXPERTS, 1)])
                    pool.drain()
                    pool.indirect_dma_start(y_rows, bass.IndirectOffsetOnAxis(ap=idx_y[:], axis=0), y[:], None,
                                            bounds_check=2047, oob_is_err=False).then_inc(s["scattered"], 16)
                    pool.wait_ge(s["scattered"], 16 * b + 16)
                    pool.sem_inc(s["stored"], 1)
                each_block(pool, body)

            @block.tensor
            def _(pe):
                def body(b):
                    pe.wait_ge(s["gathered"], 16 * b + 16)
                    for k in range(8):
                        last = nc.tensor.transpose(x_turned[:, k], x_rows[:, k * P:(k + 1) * P], c["ident"][:])
                    last.then_inc(s["x_turned_"], 1)
                    pe.wait_ge(s["x_cols_"], b + 1)
                    pe.wait_ge(s["weights"], 48 * b + 48)
                    for w, out in ((gate, gate_out), (up, up_out)):
                        for k in range(8):
                            last = nc.tensor.matmul(out[:], x_cols[:, k], w[:, k], start=(k == 0), stop=(k == 7))
                    last.then_inc(s["multiplied"], 1)
                    pe.wait_ge(s["hid_"], b + 1)
                    for k in range(4):
                        last = nc.tensor.transpose(hid_turned[:, k], hid[:, k * P:(k + 1) * P], c["ident"][:])
                    last.then_inc(s["hid_turned_"], 1)
                    pe.wait_ge(s["hid_cols_"], b + 1)
                    for half in range(2):
                        for k in range(4):
                            last = nc.tensor.matmul(y_out[:, half * BANK:(half + 1) * BANK], hid_cols[:, k],
                                                    down[:, k, half * BANK:(half + 1) * BANK], start=(k == 0), stop=(k == 3))
                    last.then_inc(s["y_made"], 1)
                each_block(pe, body)

            @block.scalar
            def _(act):
                def body(b):
                    act.wait_ge(s["multiplied"], b + 1)
                    nc.scalar.activation(silu[:], gate_out[:], ACT.Silu).then_inc(s["silued"], 1)
                    act.wait_ge(s["y_made"], b + 1)
                    act.wait_ge(s["scattered"], 16 * b)
                    nc.scalar.activation(y[:], y_out[:], ACT.Copy).then_inc(s["y_copied"], 1)
                each_block(act, body)

            @block.vector
            def _(dve):
                def body(b):
                    dve.wait_ge(s["x_turned_"], b + 1)
                    for half in range(2):
                        last = nc.vector.tensor_tensor(x_cols[:, 4 * half:4 * half + 4], x_turned[:, 4 * half:4 * half + 4],
                                                       bc(gain[:, 4 * half:4 * half + 4], 2, P), ALU.mult)
                    last.then_inc(s["x_cols_"], 1)
                    dve.wait_ge(s["silued"], b + 1)
                    nc.vector.tensor_tensor(hid[:], silu[:], up_out[:], ALU.mult).then_inc(s["hid_"], 1)
                    dve.wait_ge(s["hid_turned_"], b + 1)
                    nc.vector.tensor_copy(hid_cols[:], hid_turned[:]).then_inc(s["hid_cols_"], 1)
                each_block(dve, body)


def moe(nc, base, c, A, h, layer, u_rows, y_rows):
    gain = c[f"ffn_gain{layer}"]
    with ExitStack() as ctx:
        mem = Memory(nc, ctx, f"moe{layer}")
        scale, weight = mem.sb("scale", [P, 8]), mem.sb("weight", [P, 2, 8])
        rows_u, rows_y = mem.sb("rows_u", [P, N_BLOCKS], I32), mem.sb("rows_y", [P, N_BLOCKS], I32)
        over = mem.sb("over", [1, 17], I32)
        logits = mem.sb("logits", [P, 8, 36])
        router = mem.sb("router", [P, 8, 36])
        router_ready = mem.sem("router_ready")

        def load_router(sp):
            sp.dma_start(router[:, :, 0:4], A["router_group_w"][layer].rearrange("(k p) n -> p k n", p=P)).then_inc(router_ready, 16)
            sp.dma_start(router[:, :, 4:36], A["router_expert_w"][layer].rearrange("(k p) n -> p k n", p=P)).then_inc(router_ready, 16)

        ring_ctx = ctx.enter_context(ExitStack())
        ring = Memory(nc, ring_ctx, f"ring{layer}")
        raw, raw_ready = [ring.sb(f"raw{s}", [P, 2048]) for s in range(6)], [ring.sem(f"raw_ready{s}") for s in range(6)]

        def loads(sp):
            load_router(sp)
            for m, (name, e) in enumerate((("expert_w_gate", 0), ("expert_w_up", 0), ("expert_w_gate", 1))):
                src = A[name][layer, e].rearrange("(a k p) n -> a p k n", p=P, a=2)
                for half in range(2):
                    s = 2 * m + half
                    sp.dma_start(raw[s][:].rearrange("p (k n) -> p k n", k=4), src[half]).then_inc(raw_ready[s], 16)

        row_scales(nc, f"moe{layer}scale", c, h, scale, loads)

        def rows_of(act, tile, slot):
            return nc.scalar.activation(slot, h[:, tile], ACT.Copy, scale=scale[:, ds(tile, 1)] if not isinstance(tile, int) else scale[:, tile:tile + 1])

        def take(dve, tile, bank):
            return nc.vector.tensor_tensor(logits[:, tile], bank[:, 0:36], c["router_b"][:, layer], ALU.add)

        project_tiles(nc, f"router{layer}", c, rows_of, gain, router, 36, take, weights_ready=(router_ready, 32), store=u_rows)
        route(nc, c, layer, logits, weight, rows_u, rows_y, over)
        experts(nc, c, A, layer, gain, u_rows, y_rows, rows_u, rows_y, raw, raw_ready)
        ring_ctx.close()
        experts_over(nc, c, A, layer, gain, u_rows, y_rows, rows_u, rows_y, over)
        with ExitStack() as last:
            m2 = Memory(nc, last, f"combine{layer}")
            y = [m2.sb(f"y{j}", [P, 2, 1024]) for j in range(2)]
            y_ready, used = [m2.sem(f"y_ready{j}") for j in range(2)], m2.sem("used")
            with nc.Block() as block:

                @block.sync
                def _(sp):
                    with sp.Fori(0, 4) as pair:
                        for j in range(2):
                            sp.wait_ge(used, 2 * pair + j + 1)
                            sp.dma_start(y[j][:], y_rows[ds(256 * (2 * pair + j), 256), :].rearrange("(p k) d -> p k d", k=2)).then_inc(y_ready[j], 16)

                @block.vector
                def _(dve):
                    dve.sem_inc(used, 2)
                    with dve.Fori(0, 4) as pair:
                        for j in range(2):
                            tile = 2 * pair + j
                            dve.wait_ge(y_ready[j], 16 * pair + 16)
                            nc.vector.scalar_tensor_tensor(h[:, tile], y[j][:, 0], weight[:, 0, ds(tile, 1)], h[:, tile], ALU.mult, ALU.add)
                            dve.drain()
                            nc.vector.scalar_tensor_tensor(h[:, tile], y[j][:, 1], weight[:, 1, ds(tile, 1)], h[:, tile], ALU.mult, ALU.add)
                            dve.drain()
                            dve.sem_inc(used, 1)


def layer1(nc, base, c, A, h):
    n_q, n_kv = Q_HEADS * HEAD_DIM, KV_HEADS * HEAD_DIM
    n_qkv = n_q + 2 * n_kv
    with ExitStack() as ctx:
        mem = Memory(nc, ctx, "l1")
        scale = mem.sb("scale", [P, 8])
        qkv = mem.sb("qkv", [P, 8, n_qkv])
        cos, sin = mem.sb("cos", [P, 8, ROT // 2]), mem.sb("sin", [P, 8, ROT // 2])
        with ExitStack() as first:
            m1 = Memory(nc, first, "l1a")
            w_qkv, bias = m1.sb("w_qkv", [P, 8, n_qkv]), m1.sb("bias", [P, n_qkv])
            w_ready = m1.sem("w_ready")
            positions = m1.sb("positions", [P, 8], I32)
            pos_ready = m1.sem("pos_ready")

            def loads(sp):
                sp.dma_start(positions[:], A["positions"][0].rearrange("(t p) -> p t", p=P), allow_slow_non_contiguous=True).then_inc(pos_ready, 16)
                sp.dma_start(bias[:], broadcast_row(A["swa_b_qkv"][0], P)).then_inc(w_ready, 16)
                sp.dma_start(w_qkv[:], A["swa_w_qkv"][0].rearrange("(k p) n -> p k n", p=P)).then_inc(w_ready, 16)

            row_scales(nc, "l1scale", c, h, scale, loads)
            rotary_tables(nc, m1, positions, pos_ready, cos, sin)

            def rows_of(act, tile, slot):
                return nc.scalar.activation(slot, h[:, tile], ACT.Copy, scale=scale[:, ds(tile, 1)] if not isinstance(tile, int) else scale[:, tile:tile + 1])

            def take(dve, tile, bank):
                return nc.vector.tensor_tensor(qkv[:, tile], bank[:, 0:n_qkv], bias[:], ALU.add)

            project_tiles(nc, "qkv", c, rows_of, c["mix_gain1"], w_qkv, n_qkv, take, weights_ready=(w_ready, 32))
        with ExitStack() as second:
            m2 = Memory(nc, second, "l1b")
            w_o, bias_o = m2.sb("w_o", [P, 8, 1024]), m2.sb("bias_o", [P, 1024])
            w_ready = m2.sem("w_ready")
            window_attention(nc, c, A, qkv, cos, sin, w_o, bias_o, w_ready)

            def rows_of(act, tile, slot):
                return nc.scalar.activation(slot, qkv[:, tile, 0:n_q], ACT.Copy)

            def take(dve, tile, bank):
                nc.vector.tensor_tensor(h[:, tile], h[:, tile], bias_o[:], ALU.add)
                dve.drain()
                return nc.vector.tensor_tensor(h[:, tile], h[:, tile], bank[:], ALU.add)

            project_tiles(nc, "attn_out", c, rows_of, None, w_o, 1024, take, weights_ready=(w_ready, 32))


def rotary_tables(nc, mem, positions, pos_ready, cos, sin):
    half = ROT // 2
    pos, ang, turns = mem.sb("pos", [P, 8]), mem.sb("ang", [P, 8, half]), mem.sb("turns", [P, 8, half])
    half_sin = mem.sb("half_sin", [P, 8, half])
    reduced, sines = mem.sem("reduced"), mem.sem("sines")
    import math
    import numpy as np
    part1 = 6.28125
    part2 = float(np.float32(math.floor((2 * math.pi - part1) * 2 ** 21) / 2 ** 21))
    part3 = 2 * math.pi - part1 - part2
    to_whole = 1.5 * 2.0 ** 23
    with nc.Block() as block:

        @block.vector
        def _(dve):
            dve.wait_ge(pos_ready, 16)
            nc.vector.tensor_copy(pos[:], positions[:])
            dve.drain()
            for i in range(half):
                frequency = float(np.float32(ROPE_THETA) ** np.float32(-2.0 * i / ROT))
                nc.vector.tensor_scalar(ang[:, :, i], pos[:], frequency, None, ALU.mult)
            dve.drain()
            nc.vector.tensor_scalar(turns[:], ang[:], 1.0 / (2 * math.pi), to_whole, ALU.mult, ALU.add)
            dve.drain()
            nc.vector.tensor_scalar(turns[:], turns[:], -to_whole, None, ALU.add)
            for part in (part1, part2, part3):
                dve.drain()
                nc.vector.scalar_tensor_tensor(ang[:], turns[:], -part, ang[:], ALU.mult, ALU.add)
            dve.drain()
            nc.vector.tensor_scalar(ang[:], ang[:], math.pi * 0.9999999, -math.pi * 0.9999999, ALU.min, ALU.max)
            dve.drain()
            dve.sem_inc(reduced, 1)
            dve.wait_ge(sines, 1)
            nc.vector.tensor_tensor(cos[:], half_sin[:], half_sin[:], ALU.mult)
            dve.drain()
            nc.vector.tensor_scalar(cos[:], cos[:], -2.0, 1.0, ALU.mult, ALU.add)

        @block.scalar
        def _(act):
            act.wait_ge(reduced, 1)
            nc.scalar.activation(sin[:], ang[:], ACT.Sin)
            nc.scalar.activation(half_sin[:], ang[:], ACT.Sin, scale=0.5)
            act.drain()
            act.sem_inc(sines, 1)


def window_attention(nc, c, A, qkv, cos, sin, w_o, bias_o, w_ready):
    n_q, n_kv, half = Q_HEADS * HEAD_DIM, KV_HEADS * HEAD_DIM, ROT // 2
    n_heads = Q_HEADS + KV_HEADS
    GROUPS, PER = 4, 4
    with ExitStack() as ctx:
        mem = Memory(nc, ctx, "swa")
        rot1, rot2 = (mem.sb(x, [P, 8, n_heads, half]) for x in ("rot1", "rot2"))
        k_rows, q_rows, q_cols = mem.sb("k_rows", [P, P]), mem.sb("q_rows", [P, 1024]), mem.sb("q_cols", [P, 8, P])
        keys = mem.sb("keys", [P, KV_HEADS, 9, 2, P])
        vals = mem.sb("vals", [P, 9, n_kv])
        mask_now = mem.sb("mask_now", [P, 2, 2, P])
        masked = [mem.sb(f"masked{j}", [P, 2, 2, 2, P]) for j in range(2)]
        prob = [mem.sb(f"prob{j}", [P, PER, 2, P]) for j in range(2)]
        prob_t = mem.sb("prob_t", [P, PER, 2, P])
        top, neg_top, total, sink_part, inv = ([mem.sb(f"{x}{j}", [P, PER]) for j in range(2)]
                                               for x in ("top", "neg_top", "total", "sink_part", "inv"))
        turned = mem.ps("turned", [P, 8, P])
        scores = [mem.ps(f"scores{j}", [P, 2, 2, 2, P]) for j in range(2)]
        out = [mem.ps(f"out{j}", [P, BANK]) for j in range(2)]
        names = ("rotated", "k_rows_", "keys_turned", "keys_stored", "q_rows_", "q_turned", "q_copied", "scored", "masked_", "top_ready",
                 "prob_ready", "prob_turned", "prob_copied", "out_ready", "out_taken", "cleared")
        s = {n: mem.sem(n) for n in names}
        with nc.Block() as block:

            @block.sync
            def _(sp):
                sp.dma_start(bias_o[:], broadcast_row(A["swa_b_o"][0], P)).then_inc(w_ready, 16)
                sp.dma_start(w_o[:], A["swa_w_o"][0].rearrange("(k p) n -> p k n", p=P)).then_inc(w_ready, 16)

            @block.gpsimd
            def _(pool):
                nc.gpsimd.memset(keys[:], 0.0)
                nc.gpsimd.memset(vals[:, 0], 0.0)
                nc.gpsimd.tensor_copy(vals[:, 1:9], qkv[:, :, n_q + n_kv:])
                pool.drain()
                pool.sem_inc(s["cleared"], 1)

            @block.tensor
            def _(pe):
                pe.sem_inc(s["prob_turned"], 2)
                with pe.Fori(0, 8) as n:
                    pe.wait_ge(s["k_rows_"], n + 1)
                    pe.wait_ge(s["keys_stored"], n)
                    nc.tensor.transpose(turned[:, 0], k_rows[:], c["ident"][:]).then_inc(s["keys_turned"], 1)
                pe.wait_ge(s["keys_stored"], 8)
                pe.wait_ge(s["cleared"], 1)
                with pe.Fori(0, 8) as n:
                    pe.wait_ge(s["q_rows_"], n + 1)
                    pe.wait_ge(s["prob_copied"], GROUPS * n)
                    for k in range(8):
                        last = nc.tensor.transpose(turned[:, k], q_rows[:, k * P:(k + 1) * P], c["ident"][:])
                    last.then_inc(s["q_turned"], 1)
                    pe.wait_ge(s["q_copied"], n + 1)

                    def score(g):
                        pe.wait_ge(s["masked_"], GROUPS * n + g + 1)
                        for i in range(2):
                            chunk = 2 * g + i
                            kv = 2 * chunk // (Q_HEADS // KV_HEADS)
                            last = nc.tensor.matmul(scores[g % 2][:, i], q_cols[:, chunk], keys[:, kv, ds(n, 2)], start=True, stop=True)
                        last.then_inc(s["scored"], 1)

                    def weigh(g):
                        pe.wait_ge(s["prob_ready"], GROUPS * n + g + 3)
                        pe.wait_ge(s["prob_copied"], GROUPS * n + g)
                        for i in range(PER):
                            for b in range(2):
                                last = nc.tensor.transpose(turned[:, 2 * i + b], prob[g % 2][:, i, b], c["ident"][:])
                        last.then_inc(s["prob_turned"], 1)
                        pe.wait_ge(s["prob_copied"], GROUPS * n + g + 1)
                        pe.wait_ge(s["out_taken"], GROUPS * n + g + 1)
                        for i in range(PER):
                            kv = (PER * g + i) // (Q_HEADS // KV_HEADS)
                            for b in range(2):
                                last = nc.tensor.matmul(out[g % 2][:, i * HEAD_DIM:(i + 1) * HEAD_DIM], prob_t[:, i, b],
                                                        vals[:, n + b, kv * HEAD_DIM:(kv + 1) * HEAD_DIM], start=(b == 0), stop=(b == 1))
                        last.then_inc(s["out_ready"], 1)

                    score(0)
                    for g in range(GROUPS):
                        if g + 1 < GROUPS:
                            score(g + 1)
                        weigh(g)

            @block.scalar
            def _(act):
                act.sem_inc(s["prob_ready"], 2)
                act.wait_ge(s["rotated"], 1)
                with act.Fori(0, 8) as n:
                    act.wait_ge(s["q_turned"], n)
                    nc.scalar.activation(q_rows[:], qkv[:, n, 0:n_q], ACT.Copy).then_inc(s["q_rows_"], 1)
                    act.wait_ge(s["q_turned"], n + 1)
                    nc.scalar.activation(q_cols[:], turned[:], ACT.Copy).then_inc(s["q_copied"], 1)
                    for g in range(GROUPS):
                        j = g % 2
                        act.wait_ge(s["top_ready"], GROUPS * n + g + 1)
                        act.wait_ge(s["prob_turned"], GROUPS * n + g + 1)
                        for i in range(PER):
                            nc.scalar.activation(prob[j][:, i], masked[j][:, i // 2, :, i % 2], ACT.Exp, bias=neg_top[j][:, i:i + 1],
                                                 accum_out=total[j][:, i:i + 1])
                        nc.scalar.activation(sink_part[j][:], sink_part[j][:], ACT.Exp).then_inc(s["prob_ready"], 1)
                        act.wait_ge(s["prob_turned"], GROUPS * n + g + 3)
                        nc.scalar.activation(prob_t[:], turned[:].rearrange("p (h b) q -> p h b q", b=2), ACT.Copy).then_inc(s["prob_copied"], 1)

            @block.vector
            def _(dve):
                v = nc.vector
                dve.sem_inc(s["masked_"], 2)
                dve.sem_inc(s["out_taken"], 2)
                v.memset(mask_now[:, 0], NEG)
                v.tensor_copy(mask_now[:, 1], bc(c["swa_add"][:, 1], 1, 2))
                heads = qkv[:, :, 0:n_q + n_kv].rearrange("p t (h d) -> p t h d", d=HEAD_DIM)
                t1, t2 = heads[:, :, :, 0:half], heads[:, :, :, half:ROT]
                cos_, sin_ = bc(cos[:], 2, n_heads), bc(sin[:], 2, n_heads)
                v.tensor_tensor(rot1[:], t2, sin_, ALU.mult)
                v.tensor_tensor(rot2[:], t1, sin_, ALU.mult)
                dve.drain()
                v.tensor_tensor(t1, t1, cos_, ALU.mult)
                v.tensor_tensor(t2, t2, cos_, ALU.mult)
                dve.drain()
                v.tensor_tensor(t1, t1, rot1[:], ALU.subtract)
                v.tensor_tensor(t2, t2, rot2[:], ALU.add)
                dve.drain()
                dve.sem_inc(s["rotated"], 1)
                dve.wait_ge(s["cleared"], 1)
                with dve.Fori(0, 8) as n:
                    dve.wait_ge(s["keys_turned"], n)
                    v.tensor_copy(k_rows[:], qkv[:, n, n_q:n_q + n_kv]).then_inc(s["k_rows_"], 1)
                    dve.wait_ge(s["keys_turned"], n + 1)
                    for kv in range(KV_HEADS):
                        for odd in range(2):
                            rows = slice(HEAD_DIM * odd, HEAD_DIM * odd + HEAD_DIM)
                            last = v.tensor_copy(keys[rows, kv, n + 1, odd], turned[HEAD_DIM * kv:HEAD_DIM * (kv + 1), 0])
                    last.then_inc(s["keys_stored"], 1)
                with dve.Fori(0, 8) as n:

                    def mask(g):
                        j = g % 2
                        dve.wait_ge(s["scored"], GROUPS * n + g + 1)
                        dve.wait_ge(s["prob_ready"], GROUPS * n + g + 1)
                        v.scalar_tensor_tensor(masked[j][:].rearrange("p c s h k -> p c (s h k)"), scores[j][:].rearrange("p c s h k -> p c (s h k)"),
                                               HEAD_DIM ** -0.5, bc(mask_now[:].rearrange("p s h k -> p (s h k)"), 1, 2),
                                               ALU.mult, ALU.add).then_inc(s["masked_"], 1)
                        dve.drain()
                        v.tensor_reduce(top[j][:].rearrange("p (c h) -> p c h", c=2), masked[j][:].rearrange("p c s h k -> p c h s k"), AX.XY, ALU.max)
                        dve.drain()
                        sinks = c["sinks"][:, PER * g:PER * (g + 1)]
                        v.tensor_tensor(top[j][:], top[j][:], sinks, ALU.max)
                        dve.drain()
                        v.tensor_scalar(neg_top[j][:], top[j][:], -1.0, None, ALU.mult)
                        v.tensor_tensor(sink_part[j][:], sinks, top[j][:], ALU.subtract)
                        dve.drain()
                        dve.sem_inc(s["top_ready"], 1)

                    def take(g):
                        j = g % 2
                        dve.wait_ge(s["prob_ready"], GROUPS * n + g + 3)
                        v.tensor_tensor(inv[j][:], total[j][:], sink_part[j][:], ALU.add)
                        dve.drain()
                        v.reciprocal(inv[j][:], inv[j][:])
                        dve.drain()
                        dve.wait_ge(s["out_ready"], GROUPS * n + g + 1)
                        dst = qkv[:, n, PER * HEAD_DIM * g:PER * HEAD_DIM * (g + 1)].rearrange("p (h d) -> p h d", h=PER)
                        v.tensor_tensor(dst, out[j][:, 0:PER * HEAD_DIM].rearrange("p (h d) -> p h d", h=PER), bc(inv[j][:], 2, HEAD_DIM), ALU.mult)\
                            .then_inc(s["out_taken"], 1)

                    mask(0)
                    for g in range(GROUPS):
                        if g + 1 < GROUPS:
                            mask(g + 1)
                        take(g)
                    v.tensor_copy(mask_now[:, 0], bc(c["swa_add"][:, 0], 1, 2))
                    dve.drain()


def final_norm(nc, c, A, h, out):
    with ExitStack() as ctx:
        mem = Memory(nc, ctx, "final")
        scale, gain = mem.sb("scale", [P, 8]), mem.sb("gain", [P, 1024])
        gain_ready, made, stored = mem.sem("gain_ready"), mem.sem("made"), mem.sem("stored")

        def load_gain(sp):
            sp.dma_start(gain[:], broadcast_row(A["final_norm"], P)).then_inc(gain_ready, 16)

        row_scales(nc, "finalscale", c, h, scale, load_gain)
        with nc.Block() as block:

            @block.vector
            def _(dve):
                dve.wait_ge(gain_ready, 16)
                with dve.Fori(0, 8) as tile:
                    nc.vector.scalar_tensor_tensor(h[:, tile], h[:, tile], scale[:, ds(tile, 1)], gain[:], ALU.mult, ALU.mult).then_inc(made, 1)

            @block.sync
            def _(sp):
                with sp.Fori(0, 8) as tile:
                    sp.wait_ge(made, tile + 1)
                    sp.dma_start(out[0, ds(P * tile, P), :], h[:, tile]).then_inc(stored, 16)
                sp.wait_ge(stored, 16 * 8)


def program(nc, A, out):
    u_rows = nc.dram_tensor("u_rows", (1024, 1024), F32, kind="Internal").ap()
    y_rows = nc.dram_tensor("y_rows", (2048, 1024), F32, kind="Internal").ap()
    with ExitStack() as ctx:
        mem = Memory(nc, ctx, "base")
        c = make_constants(nc, mem, A)
        h = mem.sb("h", [P, 8, 1024])
        x_ready = mem.sem("x_ready")
        with nc.Block() as block:

            @block.sync
            def _(sp):
                sp.dma_start(h[:], A["x"][0].rearrange("(t p) d -> p t d", p=P)).then_inc(x_ready, 16)
                sp.wait_ge(x_ready, 16)

        layer0(nc, mem, c, A, h)
        moe(nc, mem, c, A, h, 0, u_rows, y_rows)
        layer1(nc, mem, c, A, h)
        moe(nc, mem, c, A, h, 1, u_rows, y_rows)
        final_norm(nc, c, A, h, out)


_INS = ["x", "positions", "mix_norm", "ffn_norm", "final_norm", "ab_w_in", "ab_conv_w", "ab_conv_b", "ml_igate_b", "ml_fgate_b",
        "ml_head_norm", "gla_w_lr_up", "gla_gate_b", "gla_head_norm", "ab_w_out", "swa_w_qkv", "swa_b_qkv", "swa_sinks", "swa_w_o",
        "swa_b_o", "router_group_w", "router_group_b", "router_expert_w", "router_expert_b", "expert_w_gate", "expert_w_up",
        "expert_w_down"]


def kernel(**inputs):
    import numpy as np
    import concourse.bacc as bacc
    from concourse.bass_utils import run_bass_kernel_spmd

    nc = bacc.Bacc("TRN2", target_bir_lowering=False, num_devices=1)
    arrays, args = {}, {}
    for name in _INS:
        a = np.ascontiguousarray(inputs[name])
        arrays[f"in_{name}_dram"] = a
        args[name] = nc.dram_tensor(f"in_{name}_dram", a.shape, mybir.dt.from_np(a.dtype), kind="ExternalInput").ap()
    out = nc.dram_tensor("out_dram", arrays["in_x_dram"].shape, F32, kind="ExternalOutput").ap()
    program(nc, args, out)
    r = run_bass_kernel_spmd(nc, [arrays], core_ids=[0])
    return r.results[0]["out_dram"]
```
